# Optimizing a Trainium2 kernel written in Bass

```python
import jax, jax.numpy as jnp
from jax import lax
import numpy as np

D_MODEL = 1024
BATCH = 1
SEQ = 1024
DEPTH = 2

GRID_W = 64
CTX_LEN = 256
HEAD_DIM = 64
EPS = 1e-6
A_HEADS = 8
A_KV_HEADS = 2
A_GROUP = A_HEADS // A_KV_HEADS
A_Q = A_HEADS * HEAD_DIM
A_KV = A_KV_HEADS * HEAD_DIM
A_IN = A_Q + 2 * A_KV
Q_BLOCK = 128
ROPE_THETA = 10000.0
ROPE_FREQS = HEAD_DIM // 4
B_GROUPS = 8
B_CH = 64
B_WIDTH = B_GROUPS * B_CH
CHUNK = 128
C_HEADS = 8
C_W = C_HEADS * HEAD_DIM
NA_MAX_ROWS = 8
NA_COLS = 16
D_CH = 512
CONV_W = 31
MIX_WIDTH = A_Q + B_WIDTH
EVEN_IN = A_IN + 2 * B_WIDTH
ODD_IN = 3 * C_W + 2 * D_CH
N_EVEN = (DEPTH + 1) // 2
N_ODD = DEPTH // 2
N_EXPERTS = 16
N_GROUPS = 4
EXPERTS_PER_GROUP = N_EXPERTS // N_GROUPS
TOPK_GROUPS = 1
TOP_K = 2
D_EXPERT = 512
MOE_BLOCK = 256

kernel_name = 'hybrid_flow_backbone'

def rms_norm(x, g):
    xf = x.astype(jnp.float32)
    y = xf * lax.rsqrt(jnp.mean(xf * xf, axis=-1, keepdims=True) + EPS)
    return (y * g.astype(jnp.float32)).astype(x.dtype)

def layer_norm(x, g, b):
    xf = x.astype(jnp.float32)
    mu = jnp.mean(xf, axis=-1, keepdims=True)
    var = jnp.mean(jnp.square(xf - mu), axis=-1, keepdims=True)
    y = (xf - mu) * lax.rsqrt(var + EPS)
    return (y * g.astype(jnp.float32) + b.astype(jnp.float32)).astype(x.dtype)

def axial_rope_tables(n_tok, dtype):
    t = jnp.arange(n_tok, dtype=jnp.int32)
    pos = jnp.stack([t // GRID_W, t % GRID_W], axis=-1).astype(jnp.float32)
    inv = ROPE_THETA ** (-jnp.arange(ROPE_FREQS, dtype=jnp.float32) / ROPE_FREQS)
    ang = pos[:, :, None] * inv
    return jnp.cos(ang).astype(dtype), jnp.sin(ang).astype(dtype)

def apply_axial_rope(x, cos, sin):
    b, s, h, _ = x.shape
    xs = x.reshape(b, s, h, 2, 2, ROPE_FREQS)
    x1, x2 = xs[..., 0, :], xs[..., 1, :]
    cs, sn = cos[None, :, None], sin[None, :, None]
    out = jnp.stack([x1 * cs - x2 * sn, x2 * cs + x1 * sn], axis=-2)
    return out.reshape(x.shape)

def dense_gqa(q, k, v):
    s = jnp.einsum('bqkgd,bskd->bkgqs', q, k, preferred_element_type=jnp.float32) * (HEAD_DIM ** -0.5)
    p = jax.nn.softmax(s, axis=-1).astype(v.dtype)
    return jnp.einsum('bkgqs,bskd->bqkgd', p, v)

def blocked_gqa(q, k, v):
    b, s = q.shape[:2]
    nb = s // Q_BLOCK
    qb = jnp.moveaxis(q.reshape(b, nb, Q_BLOCK, *q.shape[2:]), 1, 0)
    o = lax.map(lambda qi: dense_gqa(qi, k, v), qb)
    return jnp.moveaxis(o, 0, 1).reshape(q.shape)

def mixer_a(p_lat, p_ctx, q_g, k_g, need_ctx):
    b, s, _ = p_lat.shape

    def heads(p):
        lead = p.shape[:2]
        q = rms_norm(p[..., :A_Q].reshape(*lead, A_HEADS, HEAD_DIM), q_g)
        k = rms_norm(p[..., A_Q:A_Q + A_KV].reshape(*lead, A_KV_HEADS, HEAD_DIM), k_g)
        v = p[..., A_Q + A_KV:A_IN].reshape(*lead, A_KV_HEADS, HEAD_DIM)
        return q, k, v

    ql, kl, vl = heads(p_lat)
    qc, kc, vc = heads(p_ctx)
    cos, sin = axial_rope_tables(s, ql.dtype)
    ql = apply_axial_rope(ql, cos, sin)
    kl = apply_axial_rope(kl, cos, sin)
    k_all = jnp.concatenate([kc, kl], axis=1)
    v_all = jnp.concatenate([vc, vl], axis=1)
    o_lat = blocked_gqa(ql.reshape(b, s, A_KV_HEADS, A_GROUP, HEAD_DIM), k_all, v_all).reshape(b, s, A_Q)
    if not need_ctx:
        return o_lat, None
    o_ctx = dense_gqa(qc.reshape(b, -1, A_KV_HEADS, A_GROUP, HEAD_DIM), kc, vc).reshape(b, -1, A_Q)
    return o_lat, o_ctx

def chunk_spatial_gate(p, v_g, ws, bs):
    b, n_tok, _ = p.shape
    n = n_tok // CHUNK
    z = jax.nn.gelu(p)
    u, v = z[..., :B_WIDTH], z[..., B_WIDTH:]
    v = rms_norm(v.reshape(b, n, CHUNK, B_GROUPS, B_CH), v_g.reshape(B_GROUPS, B_CH))
    mixed = jnp.einsum('gts,bnsgc->bntgc', ws, v) + bs.T[:, :, None]
    return u * mixed.reshape(b, n_tok, B_WIDTH)

def neighbourhood_attention(q, k, v, k_ctx, v_ctx, rpb):
    b, s, h, dh = q.shape
    rows = s // GRID_W
    wh = min(NA_MAX_ROWS, rows)
    n_loc = wh * NA_COLS
    qg, kg, vg = (t.reshape(b, rows, GRID_W, h, dh) for t in (q, k, v))
    r = jnp.arange(rows, dtype=jnp.int32)
    row_idx = jnp.clip(r - wh // 2, 0, rows - wh)[:, None] + jnp.arange(wh, dtype=jnp.int32)[None, :]
    cc = jnp.arange(GRID_W, dtype=jnp.int32)
    col_idx = jnp.clip(cc - NA_COLS // 2, 0, GRID_W - NA_COLS)[:, None] + jnp.arange(NA_COLS, dtype=jnp.int32)[None, :]
    rpb_cols = rpb.astype(jnp.float32)[:, :, col_idx - cc[:, None] + NA_COLS - 1]
    scale = HEAD_DIM ** -0.5

    def row_block(args):
        qr, ridx, ri = args
        kr = jnp.take(kg, ridx, axis=1)[:, :, col_idx]
        vr = jnp.take(vg, ridx, axis=1)[:, :, col_idx]
        bias = jnp.transpose(rpb_cols[:, ridx - ri + NA_MAX_ROWS - 1], (0, 2, 1, 3))
        s_loc = jnp.einsum('bchd,bicjhd->bhcij', qr, kr, preferred_element_type=jnp.float32) * scale + bias
        s_ctx = jnp.einsum('bchd,bshd->bhcs', qr, k_ctx, preferred_element_type=jnp.float32) * scale
        sc = jnp.concatenate([s_loc.reshape(b, h, GRID_W, n_loc), s_ctx], axis=-1)
        p = jax.nn.softmax(sc, axis=-1).astype(v.dtype)
        p_loc = p[..., :n_loc].reshape(b, h, GRID_W, wh, NA_COLS)
        return jnp.einsum('bhcij,bicjhd->bchd', p_loc, vr) + jnp.einsum('bhcs,bshd->bchd', p[..., n_loc:], v_ctx)

    o = lax.map(row_block, (jnp.moveaxis(qg, 1, 0), row_idx, r))
    return jnp.moveaxis(o, 0, 1).reshape(b, s, h * dh)

def mixer_c(p_lat, p_ctx, q_g, k_g, rpb, need_ctx):
    def heads(p):
        lead = p.shape[:2]
        q = rms_norm(p[..., :C_W].reshape(*lead, C_HEADS, HEAD_DIM), q_g)
        k = rms_norm(p[..., C_W:2 * C_W].reshape(*lead, C_HEADS, HEAD_DIM), k_g)
        v = p[..., 2 * C_W:3 * C_W].reshape(*lead, C_HEADS, HEAD_DIM)
        return q, k, v

    ql, kl, vl = heads(p_lat)
    qc, kc, vc = heads(p_ctx)
    o_lat = neighbourhood_attention(ql, kl, vl, kc, vc, rpb)
    if not need_ctx:
        return o_lat, None
    b = qc.shape[0]
    o_ctx = dense_gqa(qc[:, :, :, None], kc, vc).reshape(b, -1, C_W)
    return o_lat, o_ctx

def conformer_conv(p, dw, dw_b, ln_g, ln_b):
    a, g = p[..., :D_CH], p[..., D_CH:]
    y = a * jax.nn.sigmoid(g)
    y = lax.conv_general_dilated(y, dw[:, None, :], window_strides=(1,),
                                 padding=[(CONV_W // 2, CONV_W // 2)],
                                 dimension_numbers=('NWC', 'WIO', 'NWC'),
                                 feature_group_count=D_CH) + dw_b
    return jax.nn.silu(layer_norm(y, ln_g, ln_b))

def moe_ffn(h, router_w, router_b, w_gate, w_up, w_down):
    t, d = h.shape
    aff = jax.nn.sigmoid(jnp.dot(h, router_w, preferred_element_type=jnp.float32))
    sel = aff + router_b.astype(jnp.float32)
    gscore = lax.top_k(sel.reshape(t, N_GROUPS, EXPERTS_PER_GROUP), 2)[0].sum(-1)
    _, gtop = lax.top_k(gscore, TOPK_GROUPS)
    gmask = jnp.any(gtop[:, :, None] == jnp.arange(N_GROUPS)[None, None, :], axis=1)
    emask = jnp.repeat(gmask, EXPERTS_PER_GROUP, axis=1)
    _, eidx = lax.top_k(jnp.where(emask, sel, -jnp.inf), TOP_K)
    w = jnp.take_along_axis(aff, eidx, axis=1)
    w = w / jnp.sum(w, axis=-1, keepdims=True)
    n_assign = t * TOP_K
    e_flat = eidx.reshape(n_assign)
    tok = jnp.repeat(jnp.arange(t, dtype=jnp.int32), TOP_K)
    gate = w.reshape(n_assign).astype(h.dtype)
    order = jnp.argsort(e_flat)
    e_s, tok_s, gate_s = e_flat[order], tok[order], gate[order]
    counts = jnp.bincount(e_flat, length=N_EXPERTS)
    start = jnp.cumsum(counts) - counts
    pcounts = (counts + MOE_BLOCK - 1) // MOE_BLOCK * MOE_BLOCK
    pend = jnp.cumsum(pcounts)
    pstart = pend - pcounts
    dest = pstart[e_s] + jnp.arange(n_assign, dtype=jnp.int32) - start[e_s]
    n_blocks = -(-n_assign // MOE_BLOCK) + N_EXPERTS
    buf = jnp.zeros((n_blocks * MOE_BLOCK, d), h.dtype).at[dest].set(h[tok_s])
    blk_e = jnp.minimum(jnp.searchsorted(pend, jnp.arange(n_blocks, dtype=jnp.int32) * MOE_BLOCK, side='right'), N_EXPERTS - 1)

    def expert_block(args):
        xb, e = args
        return (jax.nn.silu(xb @ w_gate[e]) * (xb @ w_up[e])) @ w_down[e]

    y = lax.map(expert_block, (buf.reshape(n_blocks, MOE_BLOCK, d), blk_e)).reshape(-1, d)
    return jnp.zeros_like(h).at[tok_s].add(y[dest] * gate_s[:, None])

def setup_inputs(seed: int = 0) -> dict:
    key = jax.random.key(seed)
    ks = jax.random.split(key, 32)
    f32 = jnp.float32

    def nrm(k, shape, scale):
        return jax.random.normal(k, shape, f32) * scale

    def gain(k, shape):
        return 1.0 + nrm(k, shape, 0.05)

    return {
        'x': nrm(ks[0], (BATCH, SEQ, D_MODEL), 1.0),
        'c': nrm(ks[1], (BATCH, D_MODEL), 1.0),
        'ctx': nrm(ks[2], (BATCH, CTX_LEN, D_MODEL), 1.0),
        'c_ctx': nrm(ks[3], (D_MODEL,), 1.0),
        'router_w': nrm(ks[4], (D_MODEL, N_EXPERTS), D_MODEL ** -0.5),
        'router_b': nrm(ks[5], (N_EXPERTS,), 0.01),
        'ada_w': nrm(ks[6], (DEPTH, D_MODEL, 6 * D_MODEL), 0.5 * D_MODEL ** -0.5),
        'ada_b': nrm(ks[7], (DEPTH, 6 * D_MODEL), 0.02),
        'norm1_g': gain(ks[8], (DEPTH, D_MODEL)),
        'norm2_g': gain(ks[9], (DEPTH, D_MODEL)),
        'ev_w_in': nrm(ks[10], (N_EVEN, D_MODEL, EVEN_IN), D_MODEL ** -0.5),
        'ev_w_out': nrm(ks[11], (N_EVEN, MIX_WIDTH, D_MODEL), MIX_WIDTH ** -0.5),
        'a_q_norm': gain(ks[12], (N_EVEN, HEAD_DIM)),
        'a_k_norm': gain(ks[13], (N_EVEN, HEAD_DIM)),
        'b_v_norm': gain(ks[14], (N_EVEN, B_WIDTH)),
        'b_ws': nrm(ks[15], (N_EVEN, B_GROUPS, CHUNK, CHUNK), CHUNK ** -0.5),
        'b_bs': nrm(ks[16], (N_EVEN, B_GROUPS, CHUNK), 0.02),
        'od_w_in': nrm(ks[17], (N_ODD, D_MODEL, ODD_IN), D_MODEL ** -0.5),
        'od_w_out': nrm(ks[18], (N_ODD, MIX_WIDTH, D_MODEL), MIX_WIDTH ** -0.5),
        'c_q_norm': gain(ks[19], (N_ODD, HEAD_DIM)),
        'c_k_norm': gain(ks[20], (N_ODD, HEAD_DIM)),
        'c_rpb': nrm(ks[21], (N_ODD, C_HEADS, 2 * NA_MAX_ROWS - 1, 2 * NA_COLS - 1), 0.1),
        'd_dw': nrm(ks[22], (N_ODD, CONV_W, D_CH), CONV_W ** -0.5),
        'd_dw_b': nrm(ks[23], (N_ODD, D_CH), 0.02),
        'd_ln_g': gain(ks[24], (N_ODD, D_CH)),
        'd_ln_b': nrm(ks[25], (N_ODD, D_CH), 0.02),
        'moe_w_gate': nrm(ks[26], (DEPTH, N_EXPERTS, D_MODEL, D_EXPERT), D_MODEL ** -0.5),
        'moe_w_up': nrm(ks[27], (DEPTH, N_EXPERTS, D_MODEL, D_EXPERT), D_MODEL ** -0.5),
        'moe_w_down': nrm(ks[28], (DEPTH, N_EXPERTS, D_EXPERT, D_MODEL), D_EXPERT ** -0.5),
    }

def reference(x, c, ctx, c_ctx, router_w, router_b, ada_w, ada_b, norm1_g, norm2_g,
              ev_w_in, ev_w_out, a_q_norm, a_k_norm, b_v_norm, b_ws, b_bs,
              od_w_in, od_w_out, c_q_norm, c_k_norm, c_rpb, d_dw, d_dw_b, d_ln_g, d_ln_b,
              moe_w_gate, moe_w_up, moe_w_down):
    b, s, d = x.shape
    n_ctx = ctx.shape[1]
    x_lat, x_ctx = x, ctx
    for l in range(DEPTH):
        need_ctx = l < DEPTH - 1
        mod_lat = jax.nn.silu(c) @ ada_w[l] + ada_b[l]
        mod_ctx = jax.nn.silu(c_ctx) @ ada_w[l] + ada_b[l]
        sh1, sc1, g1, sh2, sc2, g2 = jnp.split(mod_lat[:, None, :], 6, axis=-1)
        ch1, cs1, cg1, ch2, cs2, cg2 = jnp.split(mod_ctx, 6)
        h_lat = rms_norm(x_lat, norm1_g[l]) * (1.0 + sc1) + sh1
        h_ctx = rms_norm(x_ctx, norm1_g[l]) * (1.0 + cs1) + ch1
        i = l // 2
        if l % 2 == 0:
            w_in, w_out = ev_w_in[i], ev_w_out[i]
            p_lat, p_ctx = h_lat @ w_in, h_ctx @ w_in
            a_lat, a_ctx = mixer_a(p_lat[..., :A_IN], p_ctx[..., :A_IN], a_q_norm[i], a_k_norm[i], need_ctx)
            b_lat = chunk_spatial_gate(p_lat[..., A_IN:], b_v_norm[i], b_ws[i], b_bs[i])
            m_lat = jnp.concatenate([a_lat, b_lat], axis=-1)
            if need_ctx:
                b_ctx = chunk_spatial_gate(p_ctx[..., A_IN:], b_v_norm[i], b_ws[i], b_bs[i])
                m_ctx = jnp.concatenate([a_ctx, b_ctx], axis=-1)
        else:
            w_in, w_out = od_w_in[i], od_w_out[i]
            p_lat, p_ctx = h_lat @ w_in, h_ctx @ w_in
            c_lat, c_ctx_o = mixer_c(p_lat[..., :3 * C_W], p_ctx[..., :3 * C_W], c_q_norm[i], c_k_norm[i], c_rpb[i], need_ctx)
            d_lat = conformer_conv(p_lat[..., 3 * C_W:], d_dw[i], d_dw_b[i], d_ln_g[i], d_ln_b[i])
            m_lat = jnp.concatenate([c_lat, d_lat], axis=-1)
            if need_ctx:
                d_ctx = conformer_conv(p_ctx[..., 3 * C_W:], d_dw[i], d_dw_b[i], d_ln_g[i], d_ln_b[i])
                m_ctx = jnp.concatenate([c_ctx_o, d_ctx], axis=-1)
        x_lat = x_lat + g1 * (m_lat @ w_out)
        h2_lat = rms_norm(x_lat, norm2_g[l]) * (1.0 + sc2) + sh2
        if need_ctx:
            x_ctx = x_ctx + cg1 * (m_ctx @ w_out)
            h2_ctx = rms_norm(x_ctx, norm2_g[l]) * (1.0 + cs2) + ch2
            toks = jnp.concatenate([h2_lat.reshape(b * s, d), h2_ctx.reshape(b * n_ctx, d)], axis=0)
            f = moe_ffn(toks, router_w, router_b, moe_w_gate[l], moe_w_up[l], moe_w_down[l])
            f_lat = f[:b * s].reshape(b, s, d)
            x_ctx = x_ctx + cg2 * f[b * s:].reshape(b, n_ctx, d)
        else:
            f_lat = moe_ffn(h2_lat.reshape(b * s, d), router_w, router_b, moe_w_gate[l], moe_w_up[l], moe_w_down[l]).reshape(b, s, d)
        x_lat = x_lat + g2 * f_lat
    return x_lat


_drawn_inputs = setup_inputs


def setup_inputs(seed=0):
    import zlib

    import numpy as np

    out = dict(_drawn_inputs(seed))
    spreads = {}
    factors = {'a_q_norm': 8.0,
     'a_k_norm': 8.0,
     'b_bs': 3.749,
     'c_q_norm': 8.0,
     'c_k_norm': 8.0,
     'c_rpb': 28.082,
     'd_dw_b': 2.771,
     'd_ln_g': 3.401,
     'd_ln_b': 6.767}
    for name, (base, spread) in spreads.items():
        noise = np.random.default_rng([zlib.crc32(name.encode()), seed]).standard_normal(out[name].shape)
        drawn = base * np.exp(spread * noise) if base else spread * noise
        out[name] = __import__('jax').numpy.asarray(drawn.astype(out[name].dtype))
    for name, factor in factors.items():
        out[name] = (out[name] * factor).astype(out[name].dtype)
    return out
```

```python
from contextlib import ExitStack

import numpy as np

import concourse.bass as bass
from concourse import mybir

F32 = mybir.dt.float32
F32R = mybir.dt.float32r
I32 = mybir.dt.int32
ALU = mybir.AluOpType
ACT = mybir.ActivationFunctionType
AX = mybir.AxisListType

P = 128
D = 1024
KD = D // P
SEQ, CTX = 1024, 256
LT, CT = SEQ // P, CTX // P
NT = LT + CT
HD = 64
GRID_W = 64
EPS = 1e-6
A_Q, A_KV = 512, 128
A_IN = A_Q + 2 * A_KV
BW = 512
NG = 8
CONV = 31
HALO = CONV // 2
NE, NGRP, EPG = 16, 4, 4
F = 512
KF = F // P
MOD = 6 * D
SH1, SC1, G1, SH2, SC2, G2 = range(6)
BIG = 1.0e30
WIN_ROWS = 8


def max_blocks(tiles):
    return 2 * tiles + NE


class Kit:
    pass


def bc(ap, dim, n):
    v = ap.unsqueeze(dim)
    shape = list(v.shape)
    shape[dim] = n
    return v.to_broadcast(shape)


def chain(eng, sem):
    count = [0]

    def step(ins):
        count[0] += 1
        ins.then_inc(sem, 1)
        eng.wait_ge(sem, count[0])

    return step


class Phase:

    def __init__(self, nc, name):
        self.nc, self.name, self.ctx, self.sems = nc, name, ExitStack(), []

    def __enter__(self):
        self.ctx.__enter__()
        return self

    def __exit__(self, *a):
        if self.sems:
            self.nc.clear_and_free_semaphores(self.sems)
            self.nc.all_engine_barrier()
        return self.ctx.__exit__(*a)

    def sb(self, name, shape, dt=F32):
        return self.ctx.enter_context(self.nc.sbuf_tensor(f"{self.name}_{name}", shape, dt))

    def alias(self, name, other, shape, dt=F32):
        at = self.nc.lookup_mloc(other).addr
        return self.nc.alloc_sbuf_tensor_at(f"{self.name}_{name}", shape, dt, offset=at)

    def ps(self, name, shape, dt=F32):
        return self.ctx.enter_context(self.nc.psum_tensor(f"{self.name}_{name}", shape, dt))

    def sem(self, name):
        self.sems.append(self.nc.alloc_semaphore(f"{self.name}_{name}"))
        return self.sems[-1]


def as_f32(ap):
    return ap.bitcast(F32)


def modulation(nc, k, c, c_ctx, ada_w, ada_b):
    HALF = MOD // 2
    NB = HALF // 512
    with Phase(nc, "mod") as ph:
        w = [ph.sb(f"w{i}", [P, HALF]) for i in range(KD)]
        cT = ph.sb("cT", [P, KD, 2])
        sT = ph.sb("sT", [P, KD, 2])
        bias = ph.sb("bias", [2, 2, HALF])
        row = ph.sb("row", [2, 2, HALF])
        acc = ph.ps("acc", [P, NB, 512])
        c_in, b_in = ph.sem("c_in"), [ph.sem("b_in0"), ph.sem("b_in1")]
        w_in = [ph.sem(f"w_in{i}") for i in range(KD)]
        silu_done, w_used = ph.sem("silu_done"), ph.sem("w_used")
        row_ready = ph.sem("row_ready")
        stored = [ph.sem("stored0"), ph.sem("stored1")]
        with nc.Block() as block:

            @block.sync
            def _(sp):
                for v, src in enumerate((c[0, :], c_ctx)):
                    sp.dma_start(cT[:, :, v], src.rearrange("(k p) -> p k", p=P),
                                 allow_slow_non_contiguous=True).then_inc(c_in, 16)
                for r in range(4):
                    l, half = r // 2, r % 2
                    for i in range(KD):
                        if r:
                            sp.wait_ge(w_used, (r - 1) * KD + i + 1)
                        sp.dma_start(w[i][:, :], ada_w[l, i * P:(i + 1) * P, half * HALF:(half + 1) * HALF]
                                     ).then_inc(w_in[i], 16)

            @block.scalar
            def _(act):
                for r in range(4):
                    l, half = r // 2, r % 2
                    if r >= 2:
                        act.wait_ge(row_ready, r - 1)
                    for v in range(2):
                        act.dma_start(bias[v:v + 1, r % 2, :], ada_b[l:l + 1, half * HALF:(half + 1) * HALF]
                                      ).then_inc(b_in[r % 2], 16)
                    if r == 0:
                        act.wait_ge(c_in, 32)
                        nc.scalar.activation(sT[:, :, :], cT[:, :, :], ACT.Silu).then_inc(silu_done, 1)
                    act.wait_ge(row_ready, r + 1)
                    act.dma_start(k.mod_d[l, :, half * HALF:(half + 1) * HALF], row[:, r % 2, :]
                                  ).then_inc(stored[r % 2], 16)
                for p in range(2):
                    act.wait_ge(stored[p], 32)

            @block.tensor
            def _(pe):
                pe.wait_ge(silu_done, 1)
                for r in range(4):
                    if r:
                        pe.wait_ge(row_ready, r)
                    for i in range(KD):
                        pe.wait_ge(w_in[i], 16 * (r + 1))
                        for n in range(NB):
                            mm = nc.tensor.matmul(acc[0:2, n, :], sT[:, i, :], w[i][:, n * 512:(n + 1) * 512],
                                                  start=(i == 0), stop=(i == KD - 1))
                        mm.then_inc(w_used, 1)

            @block.vector
            def _(dve):
                for r in range(4):
                    dve.wait_ge(b_in[r % 2], 32 * (r // 2 + 1))
                    dve.wait_ge(w_used, KD * (r + 1))
                    if r >= 2:
                        dve.wait_ge(stored[r % 2], 16 * (r // 2))
                    nc.vector.tensor_tensor(row[:, r % 2, :], acc[0:2, :, :].rearrange("p b n -> p (b n)"),
                                            bias[:, r % 2, :], ALU.add).then_inc(row_ready, 1)


class NormStage:

    def __init__(self, ph, k, l, tiles, src_of, two_streams):
        nc = ph.nc
        self.nc, self.k, self.l, self.tiles, self.src_of = nc, k, l, tiles, src_of
        self.n = len(tiles)
        self.nv = 2 if two_streams else 1
        self.x = [ph.sb(f"x{p}", [P, D]) for p in range(2)]
        self.junk = ph.sb("junk", [P, D], mybir.dt.bfloat16)
        self.ss = ph.sb("ss", [P, 2])
        self.ms = ph.sb("ms", [P, 2])
        self.rstd = ph.sb("rstd", [P, 2])
        self.hf = ph.sb("hf", [P, KD, P])
        self.hi = [ph.sb(f"hi{p}", [P, KD, P], F32R) for p in range(2)]
        self.lo = [ph.sb(f"lo{p}", [P, KD, P], F32R) for p in range(2)]
        self.cols = ph.sb("cols", [P, 3, self.nv, KD])
        self.gain = ph.sb("gain", [P, KD])
        self.pt = [ph.ps(f"pt{h}", [P, 4, P]) for h in range(2)]
        s = ph.sem
        self.x_in = [s("x_in0"), s("x_in1")]
        self.cols_in, self.cols_ready = s("cols_in"), s("cols_ready")
        self.sq_done, self.ms_done, self.rstd_done, self.xn_done = s("sq_done"), s("ms_done"), s("rstd_done"), s("xn_done")
        self.pt_full, self.hf_ready, self.hi_done, self.lo_done = s("pt_full"), s("hf_ready"), s("hi_done"), s("lo_done")
        self.tile_used = None

    def load_columns(self, sp):
        k, l = self.k, self.l
        for v in range(self.nv):
            for j, what in enumerate((SH1, SC1)):
                sp.dma_start(self.cols[:, j, v, :], k.mod_d[l, v, what * D:(what + 1) * D].rearrange("(k p) -> p k", p=P),
                             allow_slow_non_contiguous=True).then_inc(self.cols_in, 16)
        sp.dma_start(self.gain[:, :], k.norm1_g[l, :].rearrange("(k p) -> p k", p=P),
                     allow_slow_non_contiguous=True).then_inc(self.cols_in, 16)

    def load(self, sp, i):
        if i >= 2:
            sp.wait_ge(self.pt_full, 2 * (i - 1))
        sp.dma_start(self.x[i % 2][:, :], self.src_of(self.tiles[i])).then_inc(self.x_in[i % 2], 16)

    def prepare_columns(self, dve):
        dve.wait_ge(self.cols_in, 16 * (2 * self.nv + 1))
        for v in range(self.nv):
            self.nc.vector.scalar_tensor_tensor(self.cols[:, 2, v, :], self.cols[:, 1, v, :], 1.0, self.gain[:, :],
                                                ALU.add, ALU.mult).then_inc(self.cols_ready, 1)
        dve.wait_ge(self.cols_ready, self.nv)

    def square(self, act, i):
        act.wait_ge(self.x_in[i % 2], 16 * (i // 2 + 1))
        if i:
            act.wait_ge(self.sq_done, i)
        if i >= 2:
            act.wait_ge(self.ms_done, i - 1)
        self.nc.scalar.activation(self.junk[:, :], self.x[i % 2][:, :], ACT.Square,
                                  accum_out=self.ss[:, i % 2:i % 2 + 1]).then_inc(self.sq_done, 1)

    def mean(self, dve, i):
        dve.wait_ge(self.sq_done, i + 1)
        if i >= 2:
            dve.wait_ge(self.rstd_done, i - 1)
        self.nc.vector.tensor_scalar(self.ms[:, i % 2:i % 2 + 1], self.ss[:, i % 2:i % 2 + 1], 1.0 / D, EPS,
                                     ALU.mult, ALU.add).then_inc(self.ms_done, 1)

    def root(self, pool, i):
        pool.wait_ge(self.ms_done, i + 1)
        if i >= 2:
            pool.wait_ge(self.xn_done, i - 1)
        self.nc.gpsimd.tensor_tensor(self.rstd[:, i % 2:i % 2 + 1], self.ms[:, i % 2:i % 2 + 1], self.k.mhalf[:, 0:1],
                                     ALU.pow).then_inc(self.rstd_done, 1)

    def scale(self, dve, i):
        dve.wait_ge(self.rstd_done, i + 1)
        self.nc.vector.tensor_scalar(self.x[i % 2][:, :], self.x[i % 2][:, :], self.rstd[:, i % 2:i % 2 + 1], None,
                                     ALU.mult).then_inc(self.xn_done, 1)

    def transposes(self, pe, i):
        pe.wait_ge(self.xn_done, i + 1)
        for h in range(2):
            if i:
                pe.wait_ge(self.hf_ready, 2 * (i - 1) + h + 1)
            for q in range(4):
                c = 4 * h + q
                mm = self.nc.tensor.transpose(self.pt[h][:, q, :], self.x[i % 2][:, c * P:(c + 1) * P], self.k.ident[:, :])
            mm.then_inc(self.pt_full, 1)

    def modulate(self, dve, i):
        v = 1 if self.tiles[i] >= LT else 0
        if i:
            dve.wait_ge(self.lo_done, i)
        for h in range(2):
            dve.wait_ge(self.pt_full, 2 * i + h + 1)
            for q in range(4):
                c = 4 * h + q
                ins = self.nc.vector.tensor_scalar(self.hf[:, c, :], self.pt[h][:, q, :], self.cols[:, 2, v, c:c + 1],
                                                   self.cols[:, 0, v, c:c + 1], ALU.mult, ALU.add)
            ins.then_inc(self.hf_ready, 1)

    def round_hi(self, act, i):
        act.wait_ge(self.hf_ready, 2 * (i + 1))
        if i >= 2:
            act.wait_ge(self.tile_used, i - 1)
        self.nc.scalar.activation(self.hi[i % 2][:, :, :], self.hf[:, :, :], ACT.Copy).then_inc(self.hi_done, 1)

    def rest_lo(self, pool, i):
        pool.wait_ge(self.hi_done, i + 1)
        self.nc.gpsimd.tensor_tensor(self.lo[i % 2][:, :, :], self.hf[:, :, :], as_f32(self.hi[i % 2][:, :, :]),
                                     ALU.subtract).then_inc(self.lo_done, 1)

    def product(self, out, i, w_hi, w_lo, cols):
        a, b = cols
        hi, lo = self.hi[i % 2], self.lo[i % 2]
        for c in range(KD):
            for n, (l, r) in enumerate(((hi, w_hi), (hi, w_lo), (lo, w_hi))):
                mm = self.nc.tensor.matmul(out, l[:, c, :], r[:, c, a:b], start=(c == 0 and n == 0),
                                           stop=(c == KD - 1 and n == 2))
        return mm


    def first_products(self, pe, w, outs):
        hi, lo = self.hi[0], self.lo[0]
        for c in range(KD):
            pe.wait_ge(w.lo_done, 2 * c + 2)
            for out, (a, b), signal in outs:
                for n, (l, r) in enumerate(((hi, w.hi), (hi, w.lo), (lo, w.hi))):
                    mm = self.nc.tensor.matmul(out, l[:, c, :], r[:, c, a:b], start=(c == 0 and n == 0),
                                               stop=(c == KD - 1 and n == 2))
                if c == KD - 1:
                    mm.then_inc(signal, 1)


class SplitWeights:

    def __init__(self, ph, name, chunks, cols, src_of, raw=None, ring=2):
        self.RAW = ring
        self.nc, self.cols, self.src_of = ph.nc, cols, src_of
        self.half = cols // 2
        self.pieces = [(c, h) for c in range(chunks) for h in range(2)]
        self.hi = ph.sb(f"{name}_hi", [P, chunks, cols], F32R)
        self.lo = ph.sb(f"{name}_lo", [P, chunks, cols], F32R)
        self.raw = raw or [ph.sb(f"{name}_raw{i}", [P, self.half]) for i in range(self.RAW)]
        self.raw_in = [ph.sem(f"{name}_raw_in{i}") for i in range(self.RAW)]
        self.hi_done, self.lo_done = ph.sem(f"{name}_hi_done"), ph.sem(f"{name}_lo_done")

    def load(self, sp, a=0, b=None):
        for i, (c, h) in list(enumerate(self.pieces))[a:b]:
            if i >= self.RAW:
                sp.wait_ge(self.lo_done, i - self.RAW + 1)
            sp.dma_start(self.raw[i % self.RAW][:, :], self.src_of(c)[:, h * self.half:(h + 1) * self.half]
                         ).then_inc(self.raw_in[i % self.RAW], 16)

    def round_hi(self, act, a=0, b=None):
        for i, (c, h) in list(enumerate(self.pieces))[a:b]:
            act.wait_ge(self.raw_in[i % self.RAW], 16 * (i // self.RAW + 1))
            self.nc.scalar.activation(self.hi[:, c, h * self.half:(h + 1) * self.half], self.raw[i % self.RAW][:, :],
                                      ACT.Copy).then_inc(self.hi_done, 1)

    def rest_lo(self, dve, a=0, b=None):
        for i, (c, h) in list(enumerate(self.pieces))[a:b]:
            s = slice(h * self.half, (h + 1) * self.half)
            dve.wait_ge(self.hi_done, i + 1)
            self.nc.vector.tensor_tensor(self.lo[:, c, s], self.raw[i % self.RAW][:, :], as_f32(self.hi[:, c, s]),
                                         ALU.subtract).then_inc(self.lo_done, 1)

    def wait_all(self, pe):
        pe.wait_ge(self.lo_done, len(self.pieces))


def project_even(nc, k, w_in, q_norm, k_norm, v_norm, ws, bs, rope):
    WID = A_IN + 2 * BW
    with Phase(nc, "pe") as ph:
        w = SplitWeights(ph, "w", KD, WID, lambda i: w_in[i * P:(i + 1) * P, :])
        tiles = list(range(NT))
        ns = NormStage(ph, k, 0, tiles, k.stream_in, True)
        gq = ph.sb("gq", [P, 2, HD])
        gk = ph.sb("gk", [P, 2, HD])
        tq = ph.sb("tq", [P, NT, 2, HD])
        tk = ph.sb("tk", [P, NT, 2, HD])
        gv = ph.sb("gv", [P, BW])
        wsT = ph.sb("wsT", [P, NG, P])
        bsr = ph.sb("bsr", [NG, P])
        bsT = ph.sb("bsT", [P, NG])
        sqk = ph.sb("sqk", [P, 640])
        stat = ph.sb("stat", [P, 10])
        rqk = ph.sb("rqk", [P, 10])
        qn = ph.sb("qn", [P, 640])
        r1 = ph.sb("r1", [P, 640])
        r2 = ph.sb("r2", [P, 640])
        qo = [ph.sb(f"qo{p}", [P, A_Q]) for p in range(2)]
        ko = ph.sb("ko", [P, A_KV])
        u = ph.sb("u", [P, BW])
        vz = ph.sb("vz", [P, BW])
        sqv = sqk[:, 0:BW]
        statv = ph.sb("statv", [P, NG])
        rv = ph.sb("rv", [P, NG])
        mo2 = ph.sb("mo", [P, 2, BW])
        mo = [mo2[:, 0, :], mo2[:, 1, :]]
        ws_in = mo2[:, :, :].rearrange("p a n -> p (a n)").rearrange("p (g s) -> p g s", g=NG)
        ps_q, ps_kv, ps_u, ps_v = (ph.ps(f"ps_{x}", [P, 512]) for x in "qkuv")
        ps_kT = ph.ps("ps_kT", [P, 512])
        ps_m = ph.ps("ps_m", [P, 512])
        S = {x: ph.sem(x) for x in (
            "small_in bs_in rope_ready ws_ready gemm_q gemm_kv gemm_u gemm_v sq_q stat_q rqk_done qn_done v_copied "
            "r1_done r2_done q_ready k_ready q_out0 q_out1 kT_full kT_hi kT_done u_done vz_done sqv_done statv_done rv_done "
            "vn_done mix_full m_ready m_out0 m_out1 chain_v chain_p").split()}
        q_out, m_out = (S["q_out0"], S["q_out1"]), (S["m_out0"], S["m_out1"])
        ns.tile_used = S["gemm_v"]
        SMALL = 9
        with nc.Block() as block:

            @block.sync
            def _(sp):
                ns.load_columns(sp)
                ns.load(sp, 0)
                ns.load(sp, 1)
                w.load(sp)
                for i in range(2, NT):
                    ns.load(sp, i)
                for p in range(2):
                    sp.wait_ge(q_out[p], 16 * (NT // 2))
                    sp.wait_ge(m_out[p], 16 * (NT // 2))

            @block.scalar
            def _(act):
                act.dma_start(tk[:, :, :, :], rope).then_inc(S["small_in"], 16)
                for g, src in ((gq, q_norm), (gk, k_norm)):
                    act.dma_start(g[:, 0, :], src.partition_broadcast(P)).then_inc(S["small_in"], 16)
                    act.dma_start(g[:, 1, :].rearrange("p (a b f) -> p a b f", a=2, b=2)[:, :, 0, :],
                                  src.rearrange("(a b f) -> a b f", a=2, b=2)[:, 1, :].partition_broadcast(P)
                                  ).then_inc(S["small_in"], 16)
                    act.dma_start(g[:, 1, :].rearrange("p (a b f) -> p a b f", a=2, b=2)[:, :, 1, :],
                                  src.rearrange("(a b f) -> a b f", a=2, b=2)[:, 0, :].partition_broadcast(P)
                                  ).then_inc(S["small_in"], 16)
                act.dma_start(gv[:, :], v_norm.partition_broadcast(P)).then_inc(S["small_in"], 16)
                act.dma_start(ws_in[:, :, :], ws.rearrange("g t s -> t g s")).then_inc(S["small_in"], 16)
                ns.square(act, 0)
                for i in range(NT + 1):
                    if i < NT:
                        ns.round_hi(act, i)
                    if i + 1 < NT:
                        ns.square(act, i + 1)
                    if i == 0:
                        w.round_hi(act)
                    if i:
                        j = i - 1
                        act.wait_ge(S["gemm_q"], i)
                        if j:
                            act.wait_ge(S["statv_done"], j)
                        nc.scalar.activation(sqk[:, 0:512], ps_q[:, :], ACT.Square).then_inc(S["sq_q"], 1)
                        act.wait_ge(S["gemm_kv"], i)
                        nc.scalar.activation(sqk[:, 512:640], ps_kv[:, 0:128], ACT.Square).then_inc(S["sq_q"], 1)
                        nc.scalar.activation(k.v0[:, tiles[j], :], ps_kv[:, 128:256], ACT.Copy).then_inc(S["v_copied"], 1)
                        act.wait_ge(S["gemm_u"], i)
                        if j:
                            act.wait_ge(S["m_ready"], j)
                        nc.scalar.activation(u[:, :], ps_u[:, :], ACT.Gelu_apprx_tanh).then_inc(S["u_done"], 1)
                        act.wait_ge(S["gemm_v"], i)
                        nc.scalar.activation(vz[:, :], ps_v[:, :], ACT.Gelu_apprx_tanh).then_inc(S["vz_done"], 1)
                        act.wait_ge(S["vz_done"], i)
                        act.wait_ge(S["stat_q"], i)
                        nc.scalar.activation(sqv, vz[:, :], ACT.Square).then_inc(S["sqv_done"], 1)
                        act.wait_ge(S["kT_full"], i)
                        nc.scalar.activation(k.kT0_hi[:, bass.ts(j, P)], ps_kT[:, 0:P], ACT.Copy).then_inc(S["kT_hi"], 1)
                        act.wait_ge(S["q_ready"], i)
                        act.dma_start(k.q_d[bass.ts(j, P), :], qo[j % 2][:, :]).then_inc(q_out[j % 2], 16)
                        act.wait_ge(S["m_ready"], i)
                        act.dma_start(k.m_d[bass.ts(j, P), :], mo[j % 2]).then_inc(m_out[j % 2], 16)

            @block.gpsimd
            def _(pool):
                pool.dma_start(bsr[:, :], bs).then_inc(S["bs_in"], 16)
                pool.wait_ge(S["small_in"], 16 * SMALL)
                for n, (g, t) in enumerate(((gq, tq), (gk, tk))):
                    for j in range(2):
                        if n:
                            pool.wait_ge(S["rope_ready"], 2)
                        nc.gpsimd.tensor_tensor(t[:, :, j, :], tk[:, :, j, :], bc(g[:, j, :], 1, NT),
                                                ALU.mult).then_inc(S["rope_ready"], 1)
                ns.root(pool, 0)
                pool.wait_ge(S["rope_ready"], 4)
                for i in range(NT + 1):
                    if i < NT:
                        ns.rest_lo(pool, i)
                    if i + 1 < NT:
                        ns.root(pool, i + 1)
                    if i:
                        j = i - 1
                        pool.wait_ge(S["stat_q"], i)
                        if j:
                            pool.wait_ge(S["qn_done"], j)
                        nc.gpsimd.tensor_tensor(rqk[:, :], stat[:, :], bc(k.mhalf[:, 0], 1, 10), ALU.pow
                                                ).then_inc(S["rqk_done"], 1)
                        pool.wait_ge(S["qn_done"], i)
                        if j:
                            pool.wait_ge(S["k_ready"], j)
                        nc.gpsimd.tensor_tensor(r1[:, 0:512].rearrange("p (h d) -> p h d", d=HD),
                                                qn[:, 0:512].rearrange("p (h d) -> p h d", d=HD),
                                                bc(tq[:, tiles[j], 0, :], 1, 8), ALU.mult).then_inc(S["r1_done"], 1)
                        nc.gpsimd.tensor_tensor(r1[:, 512:640].rearrange("p (h d) -> p h d", d=HD),
                                                qn[:, 512:640].rearrange("p (h d) -> p h d", d=HD),
                                                bc(tk[:, tiles[j], 0, :], 1, 2), ALU.mult).then_inc(S["r1_done"], 1)
                        pool.wait_ge(S["statv_done"], i)
                        if j:
                            pool.wait_ge(S["vn_done"], j)
                        nc.gpsimd.tensor_tensor(rv[:, :], statv[:, :], bc(k.mhalf[:, 0], 1, NG), ALU.pow
                                                ).then_inc(S["rv_done"], 1)

            @block.vector
            def _(dve):
                step = chain(dve, S["chain_v"])
                ns.prepare_columns(dve)
                ns.mean(dve, 0)
                ns.scale(dve, 0)
                for g in range(2):
                    dve.wait_ge(S["ws_ready"], g + 1)
                    src = (ps_q, ps_u)[g]
                    step(nc.vector.tensor_copy(wsT[:, 4 * g:4 * g + 4, :].rearrange("p g t -> p (g t)"), src[:, :]))
                dve.wait_ge(S["ws_ready"], 3)
                step(nc.vector.tensor_copy(bsT[:, :], ps_v[:, 0:NG]))
                dve.wait_ge(S["rope_ready"], 4)
                for i in range(NT + 1):
                    if i < NT:
                        ns.modulate(dve, i)
                    if i:
                        j = i - 1
                        dve.wait_ge(S["sq_q"], 2 * i)
                        if j:
                            dve.wait_ge(S["rqk_done"], j)
                        step(nc.vector.tensor_reduce(stat[:, :], sqk[:, :].rearrange("p (h d) -> p h d", d=HD), AX.X, ALU.add))
                        nc.vector.tensor_scalar(stat[:, :], stat[:, :], 1.0 / HD, EPS, ALU.mult, ALU.add).then_inc(S["stat_q"], 1)
                    if i + 1 < NT:
                        ns.mean(dve, i + 1)
                    if i:
                        dve.wait_ge(S["rqk_done"], i)
                        if j:
                            dve.wait_ge(S["k_ready"], j)
                        dve.wait_ge(S["v_copied"], i)
                        nc.vector.tensor_tensor(qn[:, 0:512].rearrange("p (h d) -> p h d", d=HD),
                                                ps_q[:, :].rearrange("p (h d) -> p h d", d=HD), bc(rqk[:, 0:8], 2, HD), ALU.mult)
                        nc.vector.tensor_tensor(qn[:, 512:640].rearrange("p (h d) -> p h d", d=HD),
                                                ps_kv[:, 0:128].rearrange("p (h d) -> p h d", d=HD), bc(rqk[:, 8:10], 2, HD),
                                                ALU.mult).then_inc(S["qn_done"], 1)
                        dve.wait_ge(S["qn_done"], i)
                        for a, b, t in ((0, 512, tq), (512, 640, tk)):
                            n = (b - a) // HD
                            for half in range(2):
                                o = r2[:, a:b].rearrange("p (h a b f) -> p h a b f", h=n, a=2, b=2)[:, :, :, half, :]
                                x = qn[:, a:b].rearrange("p (h a b f) -> p h a b f", h=n, a=2, b=2)[:, :, :, 1 - half, :]
                                s = t[:, tiles[j], 1, :].rearrange("p (a b f) -> p a b f", a=2, b=2)[:, :, half, :]
                                ins = nc.vector.tensor_tensor(o, x, bc(s, 1, n), ALU.mult)
                        ins.then_inc(S["r2_done"], 1)
                        dve.wait_ge(S["r2_done"], i)
                        dve.wait_ge(S["r1_done"], 2 * i)
                        if j >= 2:
                            dve.wait_ge(q_out[j % 2], 16 * (j // 2))
                        nc.vector.tensor_tensor(qo[j % 2][:, :].rearrange("p (c s d) -> p s c d", c=4, s=2),
                                                r1[:, 0:512].rearrange("p (s c d) -> p s c d", s=2, c=4),
                                                r2[:, 0:512].rearrange("p (s c d) -> p s c d", s=2, c=4), ALU.add
                                                ).then_inc(S["q_ready"], 1)
                        if j:
                            dve.wait_ge(S["kT_full"], j)
                        nc.vector.tensor_tensor(ko[:, :], r1[:, 512:640], r2[:, 512:640], ALU.add).then_inc(S["k_ready"], 1)
                    if i + 1 < NT:
                        ns.scale(dve, i + 1)
                    if i == 0:
                        w.rest_lo(dve)
                    if i:
                        dve.wait_ge(S["sqv_done"], i)
                        if j:
                            dve.wait_ge(S["rv_done"], j)
                        step(nc.vector.tensor_reduce(statv[:, :], sqv.rearrange("p (g d) -> p g d", d=HD), AX.X, ALU.add))
                        nc.vector.tensor_scalar(statv[:, :], statv[:, :], 1.0 / HD, EPS, ALU.mult, ALU.add).then_inc(S["statv_done"], 1)
                        dve.wait_ge(S["rv_done"], i)
                        v3 = vz[:, :].rearrange("p (g d) -> p g d", d=HD)
                        step(nc.vector.tensor_tensor(v3, v3, bc(rv[:, :], 2, HD), ALU.mult))
                        nc.vector.tensor_tensor(vz[:, :], vz[:, :], gv[:, :], ALU.mult).then_inc(S["vn_done"], 1)
                        dve.wait_ge(S["kT_hi"], i)
                        nc.vector.tensor_tensor(k.kT0_lo[:, bass.ts(j, P)], ps_kT[:, 0:P], as_f32(k.kT0_hi[:, bass.ts(j, P)]),
                                                ALU.subtract).then_inc(S["kT_done"], 1)
                        dve.wait_ge(S["mix_full"], i)
                        if j >= 2:
                            dve.wait_ge(m_out[j % 2], 16 * (j // 2))
                        m3 = mo[j % 2].rearrange("p (g d) -> p g d", d=HD)
                        step(nc.vector.tensor_tensor(m3, ps_m[:, :].rearrange("p (g d) -> p g d", d=HD), bc(bsT[:, :], 2, HD), ALU.add))
                        nc.vector.tensor_tensor(mo[j % 2], mo[j % 2], u[:, :], ALU.mult).then_inc(S["m_ready"], 1)

            @block.tensor
            def _(pe):
                ns.transposes(pe, 0)
                pe.wait_ge(S["small_in"], 16 * SMALL)
                pe.wait_ge(S["bs_in"], 16)
                for g in range(2):
                    for q in range(4):
                        mm = nc.tensor.transpose((ps_q, ps_u)[g][:, q * P:(q + 1) * P], ws_in[:, 4 * g + q, :], k.ident[:, :])
                    mm.then_inc(S["ws_ready"], 1)
                nc.tensor.transpose(ps_v[:, 0:NG], bsr[:, :], k.ident[0:NG, 0:NG]).then_inc(S["ws_ready"], 1)
                pe.wait_ge(S["chain_v"], 3)

                def finish(j):
                    pe.wait_ge(S["k_ready"], j + 1)
                    if j:
                        pe.wait_ge(S["kT_done"], j)
                    nc.tensor.transpose(ps_kT[:, 0:P], ko[:, :], k.ident[:, :]).then_inc(S["kT_full"], 1)
                    pe.wait_ge(S["vn_done"], j + 1)
                    if j:
                        pe.wait_ge(S["m_ready"], j)
                    for g in range(NG):
                        mm = nc.tensor.matmul(ps_m[:, g * HD:(g + 1) * HD], wsT[:, g, :], vz[:, g * HD:(g + 1) * HD],
                                              start=True, stop=True, skip_group_check=True)
                    mm.then_inc(S["mix_full"], 1)

                for j in range(NT):
                    pe.wait_ge(ns.lo_done, j + 1)
                    if j:
                        pe.wait_ge(S["qn_done"], j)
                    if j == 0:
                        ns.transposes(pe, 1)
                        ns.first_products(pe, w, ((ps_q[:, :], (0, 512), S["gemm_q"]), (ps_kv[:, 0:256], (512, 768), S["gemm_kv"]),
                                                  (ps_u[:, :], (768, 1280), S["gemm_u"]), (ps_v[:, :], (1280, 1792), S["gemm_v"])))
                        continue
                    ns.product(ps_q[:, :], j, w.hi, w.lo, (0, 512)).then_inc(S["gemm_q"], 1)
                    if j + 1 < NT:
                        ns.transposes(pe, j + 1)
                    if j:
                        pe.wait_ge(S["v_copied"], j)
                    ns.product(ps_kv[:, 0:256], j, w.hi, w.lo, (512, 768)).then_inc(S["gemm_kv"], 1)
                    if j:
                        finish(j - 1)
                        pe.wait_ge(S["u_done"], j)
                    ns.product(ps_u[:, :], j, w.hi, w.lo, (768, 1280)).then_inc(S["gemm_u"], 1)
                    if j:
                        pe.wait_ge(S["vz_done"], j)
                    ns.product(ps_v[:, :], j, w.hi, w.lo, (1280, 1792)).then_inc(S["gemm_v"], 1)
                finish(NT - 1)


def conv_weights(ph, w_in):
    return SplitWeights(ph, "w", KD, 2 * BW, lambda i: w_in[i * P:(i + 1) * P, 3 * BW:5 * BW])


def project_conv(nc, k, w, dw, dw_b, ln_g, ln_b):
    CC = BW // P
    QT = 4 * P
    PC = 2
    NQ = SEQ // QT
    with Phase(nc, "pc") as ph:
        tiles = list(range(LT))
        ns = NormStage(ph, k, 1, tiles, k.stream_mid, False)
        sg, y = ph.sb("sg", [P, BW]), ph.sb("y", [P, BW])
        yT = ph.sb("yT", [P, CC, SEQ + 2 * HALO])
        acc = [ph.sb(f"acc{q}", [P, CC, QT]) for q in range(NQ)]
        diag = [ph.sb(f"diag{c}", [P, CONV, P]) for c in range(PC)]
        eps = ph.sb("eps", [P, 1])
        sq = ph.sb("sq", [P, CC, QT])
        rstd = ph.sb("rstd_c", [P, QT])
        var = ph.sb("var", [P, QT])
        taps_in, taps = ph.sb("taps_in", [CONV, BW]), ph.sb("taps", [P, CC, CONV])
        cols = ph.sb("cols_c", [P, 3, CC])
        mean_w = ph.sb("mean_w", [P, P])
        ps_a, ps_g, ps_yT = ph.ps("ps_a", [P, BW]), ph.ps("ps_g", [P, BW]), ph.ps("ps_yT", [P, CC, P])
        ps_mu, ps_var = ph.ps("ps_mu", [P, QT]), ph.ps("ps_var", [P, QT])
        ps_c = ph.ps("ps_c", [P, QT])
        S = {x: ph.sem('conv_' + x) for x in (
            "diag_ready eps_ready prod_full prod_done taps_in taps_full taps_ready cols_in mean_ready zero_ready gemm_a gemm_g sg_done y_ready yT_full yT_done conv_done "
            "mu_full centred squared var_full var_ready root_done normed silu_done stored").split()}
        ns.tile_used = S["gemm_g"]
        DVE_CHUNKS = list(range(PC, CC))
        ND = len(DVE_CHUNKS)

        with nc.Block() as block:

            @block.sync
            def _(sp):
                ns.load_columns(sp)
                ns.load(sp, 0)
                ns.load(sp, 1)
                for i in range(2, LT):
                    ns.load(sp, i)
                for q in range(NQ):
                    sp.wait_ge(S["silu_done"], CC * (q + 1))
                    sp.dma_start(k.mT_d.rearrange("(c p) t -> p c t", p=P)[:, :, q * QT:(q + 1) * QT], acc[q][:, :, :]
                                 ).then_inc(S["stored"], 16)
                sp.wait_ge(S["stored"], 16 * NQ)

            @block.scalar
            def _(act):
                act.dma_start(taps_in[:, :], dw).then_inc(S["taps_in"], 16)
                for j, src in enumerate((dw_b, ln_g, ln_b)):
                    act.dma_start(cols[:, j, :], src.rearrange("(c p) -> p c", p=P), allow_slow_non_contiguous=True
                                  ).then_inc(S["cols_in"], 16)
                ns.square(act, 0)
                act.wait_ge(S["zero_ready"], 2)
                for i in range(LT + 1):
                    if i < LT:
                        ns.round_hi(act, i)
                    if i + 1 < LT:
                        ns.square(act, i + 1)
                    if i:
                        j = i - 1
                        act.wait_ge(S["gemm_g"], i)
                        if j:
                            act.wait_ge(S["y_ready"], j)
                        nc.scalar.activation(sg[:, :], ps_g[:, :], ACT.Sigmoid).then_inc(S["sg_done"], 1)
                        act.wait_ge(S["yT_full"], i)
                        nc.scalar.activation(yT[:, :, HALO + j * P:HALO + (j + 1) * P], ps_yT[:, :, :], ACT.Copy
                                             ).then_inc(S["yT_done"], 1)

                def take_products(q):
                    for c in range(PC):
                        act.wait_ge(S["prod_full"], PC * q + c + 1)
                        nc.scalar.activation(acc[q][:, c, :], ps_c[:, :], ACT.Identity, bias=cols[:, 0, c:c + 1]
                                             ).then_inc(S["prod_done"], 1)

                def root(q):
                    act.wait_ge(S["var_full"], q + 1)
                    if q:
                        act.wait_ge(S["root_done"], q)
                    nc.scalar.activation(var[:, :], ps_var[:, :], ACT.Sqrt, bias=eps[:, 0:1]).then_inc(S["var_ready"], 1)

                def square(q):
                    act.wait_ge(S["centred"], q + 1)
                    if q:
                        act.wait_ge(S["var_full"], q)
                    nc.scalar.activation(sq[:, :, :], acc[q][:, :, :], ACT.Square).then_inc(S["squared"], 1)

                def silu(q):
                    act.wait_ge(S["normed"], q + 1)
                    for c in range(CC):
                        nc.scalar.activation(acc[q][:, c, :], acc[q][:, c, :], ACT.Silu, bias=cols[:, 2, c:c + 1],
                                             scale=cols[:, 1, c:c + 1]).then_inc(S["silu_done"], 1)

                act.wait_ge(S["cols_in"], 48)
                act.wait_ge(S["eps_ready"], 1)
                for q in range(NQ):
                    take_products(q)
                    square(q)
                    root(q)
                    silu(q)

            @block.gpsimd
            def _(pool):
                nc.gpsimd.memset(mean_w[:, :], 1.0 / BW).then_inc(S["mean_ready"], 1)
                nc.gpsimd.memset(eps[:, :], EPS).then_inc(S["eps_ready"], 1)
                for a in (0, HALO + SEQ):
                    nc.gpsimd.memset(yT[:, :, a:a + HALO], 0.0).then_inc(S["zero_ready"], 1)
                ns.root(pool, 0)
                for i in range(LT):
                    ns.rest_lo(pool, i)
                    if i + 1 < LT:
                        ns.root(pool, i + 1)
                    if i < PC:
                        pool.wait_ge(S["taps_ready"], 1)
                        nc.gpsimd.tensor_tensor(diag[i][:, :, :], bc(k.ident[:, :], 1, CONV), bc(taps[:, i, :], 2, P), ALU.mult
                                                ).then_inc(S["diag_ready"], 1)

            @block.vector
            def _(dve):
                step_count = [0]
                EARLY = 6

                def convolve(q, a, b):
                    dve.wait_ge(S["yT_done"], min(4 * q + 5, LT))
                    for t in range(a, b):
                        for c in DVE_CHUNKS:
                            src = yT[:, c, q * QT + t:q * QT + t + QT]
                            if t == 0:
                                ins = nc.vector.tensor_scalar(acc[q][:, c, :], src, taps[:, c, 0:1], cols[:, 0, c:c + 1],
                                                              ALU.mult, ALU.add)
                            else:
                                dve.wait_ge(S["conv_done"], step_count[0] - ND + 1)
                                ins = nc.vector.scalar_tensor_tensor(acc[q][:, c, :], src, taps[:, c, t:t + 1], acc[q][:, c, :],
                                                                     ALU.mult, ALU.add)
                            ins.then_inc(S["conv_done"], 1)
                            step_count[0] += 1

                def centre(q):
                    dve.wait_ge(S["mu_full"], q + 1)
                    nc.vector.tensor_tensor(acc[q][:, :, :], acc[q][:, :, :], bc(ps_mu[:, :], 1, CC), ALU.subtract
                                            ).then_inc(S["centred"], 1)

                def norm(q):
                    dve.wait_ge(S["var_ready"], q + 1)
                    if q:
                        dve.wait_ge(S["normed"], q)
                    nc.vector.reciprocal(rstd[:, :], var[:, :]).then_inc(S["root_done"], 1)
                    dve.wait_ge(S["root_done"], q + 1)
                    dve.wait_ge(S["squared"], q + 1)
                    nc.vector.tensor_tensor(acc[q][:, :, :], acc[q][:, :, :], bc(rstd[:, :], 1, CC), ALU.mult
                                            ).then_inc(S["normed"], 1)

                ns.prepare_columns(dve)
                ns.mean(dve, 0)
                ns.scale(dve, 0)
                dve.wait_ge(S["taps_full"], 1)
                nc.vector.tensor_copy(taps[:, :, :], ps_a[:, 0:CC * 32].rearrange("p (c t) -> p c t", c=CC)[:, :, 0:CONV]
                                      ).then_inc(S["taps_ready"], 1)
                dve.wait_ge(S["taps_ready"], 1)
                dve.wait_ge(S["cols_in"], 48)
                dve.wait_ge(S["zero_ready"], 2)
                for i in range(LT + 1):
                    if i < LT:
                        ns.modulate(dve, i)
                    if i + 1 < LT:
                        ns.mean(dve, i + 1)
                    if i:
                        dve.wait_ge(S["sg_done"], i)
                        if i > 1:
                            dve.wait_ge(S["yT_full"], i - 1)
                        nc.vector.tensor_tensor(y[:, :], ps_a[:, :], sg[:, :], ALU.mult).then_inc(S["y_ready"], 1)
                    if i + 1 < LT:
                        ns.scale(dve, i + 1)
                    if i == LT - 1:
                        convolve(0, 0, EARLY)
                convolve(0, EARLY, CONV)
                convolve(1, 0, CONV // 2)
                centre(0)
                norm(0)
                convolve(1, CONV // 2, CONV)
                centre(1)
                norm(1)

            @block.tensor
            def _(pe):
                ns.transposes(pe, 0)
                pe.wait_ge(S["taps_in"], 16)
                for c in range(CC):
                    mm = nc.tensor.transpose(ps_a[:, c * 32:c * 32 + CONV], taps_in[:, c * P:(c + 1) * P],
                                             k.ident[0:CONV, 0:CONV])
                mm.then_inc(S["taps_full"], 1)
                w.wait_all(pe)

                def transpose_y(j):
                    pe.wait_ge(S["y_ready"], j + 1)
                    if j:
                        pe.wait_ge(S["yT_done"], j)
                    for c in range(CC):
                        mm = nc.tensor.transpose(ps_yT[:, c, :], y[:, c * P:(c + 1) * P], k.ident[:, :])
                    mm.then_inc(S["yT_full"], 1)

                for j in range(LT):
                    if j + 1 < LT:
                        ns.transposes(pe, j + 1)
                    pe.wait_ge(ns.lo_done, j + 1)
                    if j == 0:
                        pe.wait_ge(S["taps_ready"], 1)
                    else:
                        pe.wait_ge(S["sg_done"], j)
                    ns.product(ps_g[:, :], j, w.hi, w.lo, (BW, 2 * BW)).then_inc(S["gemm_a"], 1)
                    if j:
                        pe.wait_ge(S["y_ready"], j)
                    ns.product(ps_a[:, :], j, w.hi, w.lo, (0, BW)).then_inc(S["gemm_g"], 1)
                    if j:
                        transpose_y(j - 1)
                transpose_y(LT - 1)

                def total(out, src, sem):
                    for c in range(CC):
                        mm = nc.tensor.matmul(out, mean_w[:, :], src[:, c, :], start=(c == 0), stop=(c == CC - 1))
                    mm.then_inc(S[sem], 1)

                pe.wait_ge(S["mean_ready"], 1)
                pe.wait_ge(S["diag_ready"], PC)
                for q in range(NQ):
                    pe.wait_ge(S["yT_done"], min(4 * q + 5, LT))
                    for c in range(PC):
                        if q or c:
                            pe.wait_ge(S["prod_done"], PC * q + c)
                        for t in range(CONV):
                            mm = nc.tensor.matmul(ps_c[:, :], diag[c][:, t, :], yT[:, c, q * QT + t:q * QT + t + QT],
                                                  start=(t == 0), stop=(t == CONV - 1))
                        mm.then_inc(S["prod_full"], 1)
                    pe.wait_ge(S["conv_done"], ND * CONV * (q + 1))
                    pe.wait_ge(S["prod_done"], PC * (q + 1))
                    if q:
                        pe.wait_ge(S["centred"], q)
                    total(ps_mu[:, :], acc[q], "mu_full")
                    pe.wait_ge(S["squared"], q + 1)
                    if q:
                        pe.wait_ge(S["var_ready"], q)
                    total(ps_var[:, :], sq, "var_full")


def project_odd(nc, k, w_in, q_norm, k_norm, rpb):
    H = BW // HD
    with Phase(nc, "po") as ph:
        w = SplitWeights(ph, "w", KD, 3 * BW, lambda i: w_in[i * P:(i + 1) * P, 0:3 * BW])
        tiles = list(range(NT))
        ns = NormStage(ph, k, 1, tiles, k.stream_mid, True)
        gains = ph.sb("gains", [P, 2, HD])
        bias_rows = ph.sb("bias_rows", [8 * 15, P])
        sq = ph.sb("sq", [P, 2 * BW])
        stat, r = ph.sb("stat", [P, 2 * H]), ph.sb("r", [P, 2 * H])
        qk = ph.sb("qk", [P, 2 * BW])
        ps_q, ps_k, ps_v, ps_kT = (ph.ps(f"ps_{x}", [P, BW]) for x in ("q", "k", "v", "kT"))
        S = {x: ph.sem('head_' + x) for x in ("gains_in gemm_q gemm_k gemm_v sq_done sums_done stat_done r_done qk_done q_ready k_ready "
                                    "v_copied rows_zero rows_in rows_out q_out kT_full kT_hi kT_done").split()}
        ns.tile_used = S["gemm_v"]

        def first(j):
            return 0 if j < LT else BW

        def per_head(ap):
            return ap.rearrange("p (h d) -> p h d", d=HD)

        with nc.Block() as block:

            @block.sync
            def _(sp):
                ns.load_columns(sp)
                ns.load(sp, 0)
                ns.load(sp, 1)
                for n, src in enumerate((q_norm, k_norm)):
                    sp.dma_start(gains[:, n, :], src.partition_broadcast(P)).then_inc(S["gains_in"], 16)
                sp.wait_ge(S["rows_zero"], 1)
                sp.dma_start(bias_rows[:, P // 2 - 16:P // 2 + 15], rpb.rearrange("h r c -> (h r) c")).then_inc(S["rows_in"], 16)
                w.load(sp)
                for i in range(2, NT):
                    ns.load(sp, i)
                sp.wait_ge(S["rows_in"], 16)
                sp.dma_start(k.rpb_d.rearrange("h r c j -> (h r) c j"), bc(bias_rows[:, :], 1, GRID_W)).then_inc(S["rows_out"], 16)
                sp.wait_ge(S["rows_out"], 16)
                sp.wait_ge(S["q_out"], 16 * LT)

            @block.scalar
            def _(act):
                ns.square(act, 0)
                for i in range(NT + 1):
                    if i < NT:
                        ns.round_hi(act, i)
                    if i + 1 < NT:
                        ns.square(act, i + 1)
                    if i == 0:
                        w.round_hi(act)
                    if i:
                        j = i - 1
                        if j:
                            act.wait_ge(S["sums_done"], j)
                        if j < LT:
                            act.wait_ge(S["gemm_q"], i)
                            nc.scalar.activation(sq[:, 0:BW], ps_q[:, :], ACT.Square).then_inc(S["sq_done"], 1)
                        act.wait_ge(S["gemm_k"], i)
                        nc.scalar.activation(sq[:, BW:], ps_k[:, :], ACT.Square).then_inc(S["sq_done"], 1)
                        act.wait_ge(S["gemm_v"], i)
                        nc.scalar.activation(k.v1[:, j, :], ps_v[:, :], ACT.Copy).then_inc(S["v_copied"], 1)
                        act.wait_ge(S["kT_full"], i)
                        nc.scalar.activation(k.kT1_hi[:, :, j * P:(j + 1) * P], ps_kT[:, :].rearrange("p (c t) -> p c t", c=4),
                                             ACT.Copy).then_inc(S["kT_hi"], 1)
                        if j < LT:
                            act.wait_ge(S["q_ready"], i)
                            act.dma_start(k.q_d[j * P:(j + 1) * P, :], qk[:, 0:BW]).then_inc(S["q_out"], 16)

            @block.gpsimd
            def _(pool):
                nc.gpsimd.memset(bias_rows[:, :], 0.0).then_inc(S["rows_zero"], 1)
                ns.root(pool, 0)
                pool.wait_ge(S["gains_in"], 32)
                for i in range(NT + 1):
                    if i < NT:
                        ns.rest_lo(pool, i)
                    if i + 1 < NT:
                        ns.root(pool, i + 1)
                    if i:
                        j = i - 1
                        h0 = first(j) // HD
                        pool.wait_ge(S["stat_done"], i)
                        if j:
                            pool.wait_ge(S["qk_done"], j)
                        nc.gpsimd.tensor_tensor(r[:, h0:], stat[:, h0:], bc(k.mhalf[:, 0], 1, 2 * H - h0), ALU.pow
                                                ).then_inc(S["r_done"], 1)
                        pool.wait_ge(S["qk_done"], i)
                        if j < LT:
                            nc.gpsimd.tensor_tensor(per_head(qk[:, 0:BW]), per_head(qk[:, 0:BW]), bc(gains[:, 0, :], 1, H),
                                                    ALU.mult).then_inc(S["q_ready"], 1)

            @block.vector
            def _(dve):
                ns.prepare_columns(dve)
                ns.mean(dve, 0)
                ns.scale(dve, 0)
                dve.wait_ge(S["gains_in"], 32)
                for i in range(NT + 1):
                    if i < NT:
                        ns.modulate(dve, i)
                    if i + 1 < NT:
                        ns.mean(dve, i + 1)
                        ns.scale(dve, i + 1)
                    if i == 0:
                        w.rest_lo(dve)
                    if i:
                        j = i - 1
                        c0 = first(j)
                        h0 = c0 // HD
                        dve.wait_ge(S["sq_done"], 2 * min(i, LT) + max(i - LT, 0))
                        if j:
                            dve.wait_ge(S["r_done"], j)
                        nc.vector.tensor_reduce(stat[:, h0:], per_head(sq[:, c0:]), AX.X, ALU.add).then_inc(S["sums_done"], 1)
                        dve.wait_ge(S["sums_done"], i)
                        nc.vector.tensor_scalar(stat[:, h0:], stat[:, h0:], 1.0 / HD, EPS, ALU.mult, ALU.add
                                                ).then_inc(S["stat_done"], 1)
                        dve.wait_ge(S["r_done"], i)
                        if j:
                            dve.wait_ge(S["kT_full"], j)
                        if 0 < j < LT:
                            dve.wait_ge(S["q_out"], 16 * j)
                        if j < LT:
                            nc.vector.tensor_tensor(per_head(qk[:, 0:BW]), per_head(ps_q[:, :]), bc(r[:, 0:H], 2, HD), ALU.mult)
                        nc.vector.tensor_tensor(per_head(qk[:, BW:]), per_head(ps_k[:, :]), bc(r[:, H:], 2, HD), ALU.mult
                                                ).then_inc(S["qk_done"], 1)
                        dve.wait_ge(S["qk_done"], i)
                        nc.vector.tensor_tensor(per_head(qk[:, BW:]), per_head(qk[:, BW:]), bc(gains[:, 1, :], 1, H), ALU.mult
                                                ).then_inc(S["k_ready"], 1)
                        dve.wait_ge(S["kT_hi"], i)
                        nc.vector.tensor_tensor(k.kT1_lo[:, :, j * P:(j + 1) * P], ps_kT[:, :].rearrange("p (c t) -> p c t", c=4),
                                                as_f32(k.kT1_hi[:, :, j * P:(j + 1) * P]), ALU.subtract).then_inc(S["kT_done"], 1)

            @block.tensor
            def _(pe):
                ns.transposes(pe, 0)

                def transpose_k(j):
                    pe.wait_ge(S["k_ready"], j + 1)
                    if j:
                        pe.wait_ge(S["kT_done"], j)
                    for c in range(4):
                        mm = nc.tensor.transpose(ps_kT[:, c * P:(c + 1) * P], qk[:, BW + c * P:BW + (c + 1) * P], k.ident[:, :])
                    mm.then_inc(S["kT_full"], 1)

                for j in range(NT):
                    pe.wait_ge(ns.lo_done, j + 1)
                    if j:
                        pe.wait_ge(S["qk_done"], j)
                    if j == 0:
                        ns.transposes(pe, 1)
                        ns.first_products(pe, w, ((ps_q[:, :], (0, BW), S["gemm_q"]), (ps_k[:, :], (BW, 2 * BW), S["gemm_k"]),
                                                  (ps_v[:, :], (2 * BW, 3 * BW), S["gemm_v"])))
                        continue
                    if j < LT:
                        ns.product(ps_q[:, :], j, w.hi, w.lo, (0, BW)).then_inc(S["gemm_q"], 1)
                    transpose_k(j - 1)
                    if j + 1 < NT:
                        ns.transposes(pe, j + 1)
                    ns.product(ps_k[:, :], j, w.hi, w.lo, (BW, 2 * BW)).then_inc(S["gemm_k"], 1)
                    pe.wait_ge(S["v_copied"], j)
                    ns.product(ps_v[:, :], j, w.hi, w.lo, (2 * BW, 3 * BW)).then_inc(S["gemm_v"], 1)
                transpose_k(NT - 1)


def key_plan(l, tile):
    if l == 0:
        return [(0, NT)] if tile < LT else [(LT, CT)]
    if tile < 2:
        return [(0, 4), (LT, CT)]
    if tile >= LT - 2:
        return [(LT - 4, 4), (LT, CT)]
    return [(tile - 2, 5), (LT, CT)]


def bias_group(tile):
    return (0, 5) if tile < 2 else (1, 3) if tile < LT - 2 else (2, 1)


class AttendPlan:

    def __init__(self, l):
        self.tiles = list(range(NT)) if l == 0 else list(range(LT))
        self.units = [(i, h) for i in range(len(self.tiles)) for h in range(8)]
        self.chunks, self.pt = {}, {}
        uses_s, uses_t, next_s, next_t = [0] * 3, [0] * 2, 0, 0
        self.events = []

        def bank_s(u):
            nonlocal next_s
            i = self.units[u][0]
            runs, out, at = key_plan(l, self.tiles[i]), [], 0
            for first, n in runs:
                size = 512 if l == 0 else n * P // 2 if n > CT else n * P
                for a in range(0, n * P, size):
                    w = min(size, n * P - a)
                    out.append((next_s, uses_s[next_s], first * P + a, w, at, l == 1 and n > CT))
                    uses_s[next_s] += 1
                    next_s = (next_s + 1) % 3
                    at += w
            self.chunks[u] = out

        def bank_t(key, n):
            nonlocal next_t
            self.pt[key] = []
            for _ in range(n):
                self.pt[key].append((next_t, uses_t[next_t]))
                uses_t[next_t] += 1
                next_t = (next_t + 1) % 2

        def event(what, *a):
            if what == 'qk':
                bank_s(a[0])
            elif what == 'probs':
                n = sum(c for _, c in key_plan(l, self.tiles[self.units[a[0]][0]]))
                bank_t((what, *a), -(-n // 4))
            elif what == 'q':
                bank_t((what, *a), 1)
            elif what == 'mixed':
                bank_t((what, *a), 2 if l == 0 else 1)
            elif what == 'h':
                bank_t((what, *a), 2)
            self.events.append((what, *a))

        nu, nt = len(self.units), len(self.tiles)
        event('q', 0)
        event('qk', 0)
        event('qk', 1)
        for u in range(nu):
            i, h = self.units[u]
            if h == 0 and i >= 2:
                event('router', i - 2)
            if u + 2 < nu:
                event('qk', u + 2)
            event('probs', u)
            if u:
                event('pv', u - 1)
            if i:
                for what in {0: [('heads', i - 1)], 1: [('mixed', i - 1)], 2: [('out', i - 1, 0)], 3: [('out', i - 1, 1)],
                             4: [('square', i - 1)], 5: [('mean', i - 1)], 6: [('norm', i - 1)], 7: [('h', i - 1)]}[h]:
                    event(*what)
            if h == 5 and i + 1 < nt:
                event('q', i + 1)
        event('pv', nu - 1)
        if nt >= 2:
            event('router', nt - 2)
        for what in (('heads',), ('mixed',), ('out', 0), ('out', 1), ('square',), ('mean',), ('norm',), ('h',), ('router',)):
            event(what[0], nt - 1, *what[1:])


def attend(nc, k, l, w_out, colmask, rowmask):
    plan = AttendPlan(l)
    tiles, units, nt = plan.tiles, plan.units, len(plan.tiles)
    nv = 2 if l == 0 else 1
    width = (NT if l == 0 else 7) * P
    with Phase(nc, f"at{l}") as ph:
        x = ph.sb("x", [P, D])
        w = SplitWeights(ph, "w", KD, D, lambda i: w_out[i * P:(i + 1) * P, :], raw=[x[:, 0:512], x[:, 512:]])
        s = [ph.sb(f"s{i}", [P, width]) for i in range(3)]
        pT = [ph.sb(f"pT{i}", [P, width // P, P]) for i in range(2)]
        mx, nmx = ph.sb("mx", [P, 3, 3]), ph.sb("nmx", [P, 3])
        sums, rsums = ph.sb("sums", [P, 2, 8]), ph.sb("rsums", [P, 8])
        q_in_sb = ph.sb("q_in_sb", [P, A_Q])
        qT_hi = [ph.sb(f"qT_hi{i}", [P, 4, P], F32R) for i in range(2)]
        qT_lo = [ph.sb(f"qT_lo{i}", [P, 4, P], F32R) for i in range(2)]
        m = ph.sb("m", [P, D])
        aT_hi = ph.sb("aT_hi", [P, KD, P], F32R)
        aT_lo = ph.sb("aT_lo", [P, KD, P], F32R)
        tmp = ph.sb("tmp", [P, 512])
        junk = ph.sb("junk", [P, D], mybir.dt.bfloat16)
        ss, ms, rstd = ph.sb("ss", [P, 1]), ph.sb("ms", [P, 1]), ph.sb("rstd", [P, 1])
        gate = ph.sb("gate", [P, nv, D])
        scale2 = ph.sb("scale2", [P, nv, D])
        shift2 = ph.sb("shift2", [P, nv, D])
        rw = ph.sb("rw", [P, KD, NE])
        rw_hi, rw_lo = ph.sb("rw_hi", [P, KD, NE], F32R), ph.sb("rw_lo", [P, KD, NE], F32R)
        if l == 0:
            zero = ph.sb("zero", [P, D])
        if l == 1:
            table = ph.sb("table", [P, 8, 10 * GRID_W])
            cmask, rmask = ph.sb("cmask", [P, GRID_W]), ph.sb("rmask", [P, 10])
        ps_s = [ph.ps(f"ps_s{i}", [P, 512]) for i in range(3)]
        ps_t = [ph.ps(f"ps_t{i}", [P, 4, P]) for i in range(2)]
        ps_o = [ph.ps(f"ps_o{i}", [P, 512]) for i in range(2)]
        ps_g = ph.ps("ps_g", [P, 512])
        S = {n: ph.sem(n) for n in (
            "q_in m_in x_in rows_in rows_ready rw_in rw_hi_done rw_ready max_done exp_done pv_done q_hi q_ready heads_done "
            "rsum_done m_hi m_ready g_full g_read tmp_ready x_added x_stored sq_done ms_done rstd_done "
            "n_scaled h_ready h_stored h_hi h_lo router_full router_done chain mask_in zero_ready zeroed").split()}
        s_full = [ph.sem(f"s_full{i}") for i in range(3)]
        s_read = [ph.sem(f"s_read{i}") for i in range(3)]
        t_full = [ph.sem(f"t_full{i}") for i in range(2)]
        t_read = [ph.sem(f"t_read{i}") for i in range(2)]
        if l == 1:
            table_in = [ph.sem(f"table_in{h}") for h in range(8)]
            table_ready = [ph.sem(f"table_ready{h}") for h in range(8)]

        W_TURNS = 5
        W_STEP = -(-len(w.pieces) // W_TURNS)

        def kT(part, h, a, n):
            if l == 0:
                t = (k.kT0_hi, k.kT0_lo)[part]
                return t[(h // 4) * HD:(h // 4 + 1) * HD, a:a + n]
            t = (k.kT1_hi, k.kT1_lo)[part]
            return t[(h % 2) * HD:(h % 2 + 1) * HD, h // 2, a:a + n]

        def qT(part, i, h):
            t = (qT_hi, qT_lo)[part][i % 2]
            half, c = (h // 4, h % 4) if l == 0 else (h % 2, h // 2)
            return t[half * HD:(half + 1) * HD, c, :]

        def values(kt, h):
            return k.v0[:, kt, (h // 4) * HD:(h // 4 + 1) * HD] if l == 0 else k.v1[:, kt, h * HD:(h + 1) * HD]

        def key_tiles(u):
            return [t for first, n in key_plan(l, tiles[units[u][0]]) for t in range(first, first + n)]

        def stream(i):
            return 1 if tiles[i] >= LT else 0

        def after_probs(eng, u):
            for bank, n in plan.pt[('probs', u)]:
                eng.wait_ge(t_full[bank], n + 1)

        with nc.Block() as block:

            @block.sync
            def _(sp):
                def load_q(i):
                    if i:
                        bank, n = plan.pt[('q', i - 1)][0]
                        sp.wait_ge(t_full[bank], n + 1)
                    sp.dma_start(q_in_sb[:, :], k.q_d[tiles[i] * P:(tiles[i] + 1) * P, :]).then_inc(S["q_in"], 16)

                load_q(0)
                for v in range(nv):
                    for dst, what in ((gate, G1), (scale2, SC2), (shift2, SH2)):
                        sp.dma_start(dst[:, v, :], k.mod_d[l, v, what * D:(what + 1) * D].partition_broadcast(P)
                                     ).then_inc(S["rows_in"], 16)
                sp.dma_start(m[:, :], k.norm2_g[l, :].partition_broadcast(P)).then_inc(S["rows_in"], 16)
                sp.dma_start(rw[:, :, :], k.router_w.rearrange("(c p) e -> p c e", p=P)).then_inc(S["rw_in"], 16)
                w.load(sp)
                load_q(1)
                for i in range(nt):
                    t = tiles[i]
                    if i == 0:
                        sp.wait_ge(w.lo_done, len(w.pieces))
                    else:
                        sp.wait_ge(S["x_stored"], 16 * i)
                        sp.wait_ge(S["n_scaled"], i)
                    sp.dma_start(x[:, :], (k.stream_in if l == 0 else k.stream_mid)(t)).then_inc(S["x_in"], 16)
                    if i:
                        for bank, n in plan.pt[('h', i - 1)]:
                            sp.wait_ge(t_full[bank], n + 1)
                        sp.wait_ge(S["h_stored"], 16 * i)
                    else:
                        sp.wait_ge(S["rows_ready"], nv)
                    if l == 0:
                        sp.dma_start(m[:, 512:], k.m_d[t * P:(t + 1) * P, :]).then_inc(S["m_in"], 16)
                    else:
                        sp.dma_start(m[:, 512:].rearrange("p (c t) -> p c t", c=4),
                                     k.mT_d.rearrange("(c p) t -> p c t", p=P)[:, :, t * P:(t + 1) * P]).then_inc(S["m_in"], 16)
                    if i + 2 < nt:
                        load_q(i + 2)
                    sp.wait_ge(S["x_added"], 2 * (i + 1))
                    sp.dma_start(k.x_d[t * P:(t + 1) * P, :], x[:, :]).then_inc(S["x_stored"], 16)
                    sp.wait_ge(S["h_ready"], i + 1)
                    sp.dma_start(k.h_d[t * P:(t + 1) * P, :], m[:, :]).then_inc(S["h_stored"], 16)
                sp.wait_ge(S["x_stored"], 16 * nt)
                sp.wait_ge(S["h_stored"], 16 * nt)

            @block.scalar
            def _(act):
                def load_table(h, g):
                    first = (5, 3, 1)[g]
                    src = k.rpb_d
                    for a in range(2):
                        ap = bass.AP(src.tensor, (h * 15 + first - a) * GRID_W * P + P // 2 - 1,
                                     [[P - 1, GRID_W], [GRID_W * P, 10], [1, GRID_W]])
                        act.dma_start(table[a * GRID_W:(a + 1) * GRID_W, h, :].rearrange("p (s c) -> p s c", s=10), ap
                                      ).then_inc(table_in[h], 16)

                if l == 1:
                    act.dma_start(cmask[:, :], colmask).then_inc(S["mask_in"], 16)
                    act.dma_start(rmask[:, :], rowmask).then_inc(S["mask_in"], 16)
                    for h in range(8):
                        load_table(h, 0)
                act.wait_ge(S["rw_in"], 16)
                nc.scalar.activation(rw_hi[:, :, :], rw[:, :, :], ACT.Copy).then_inc(S["rw_hi_done"], 1)
                for ev in plan.events:
                    what, i = ev[0], ev[1]
                    if what == 'probs' and i < W_TURNS:
                        w.round_hi(act, i * W_STEP, (i + 1) * W_STEP)
                    if what == 'qk':
                        u, (i, h) = i, units[i]
                        act.wait_ge(S["max_done"], u + 1)
                        if h == 0 and i >= 2:
                            act.wait_ge(S["heads_done"], i - 1)
                        n = sum(c[3] for c in plan.chunks[u])
                        nc.scalar.activation(s[u % 3][:, 0:n], s[u % 3][:, 0:n], ACT.Exp, bias=nmx[:, u % 3:u % 3 + 1],
                                             accum_out=sums[:, i % 2, h:h + 1]).then_inc(S["exp_done"], 1)
                        if l == 1 and i + 1 < nt and bias_group(tiles[i])[0] != bias_group(tiles[i + 1])[0]:
                            load_table(h, bias_group(tiles[i + 1])[0])
                    elif what == 'probs':
                        u = i
                        for j, (bank, n) in enumerate(plan.pt[ev]):
                            if bank:
                                continue
                            act.wait_ge(t_full[bank], n + 1)
                            if u >= 2:
                                act.wait_ge(S["pv_done"], u - 1)
                            c = min(4, len(key_tiles(u)) - 4 * j)
                            nc.scalar.activation(pT[u % 2][:, 4 * j:4 * j + c, :], ps_t[bank][:, 0:c, :], ACT.Copy
                                                 ).then_inc(t_read[bank], 1)
                    elif what == 'q':
                        bank, n = plan.pt[ev][0]
                        act.wait_ge(t_full[bank], n + 1)
                        if i >= 2:
                            last = 8 * (i - 1) - 1
                            b2, n2 = plan.chunks[last][-1][:2]
                            act.wait_ge(s_full[b2], n2 + 1)
                        nc.scalar.activation(qT_hi[i % 2][:, :, :], ps_t[bank][:, :, :], ACT.Copy, scale=HD ** -0.5
                                             ).then_inc(S["q_hi"], 1)
                    elif what == 'mixed':
                        if i:
                            act.wait_ge(S["router_full"], i)
                        for j, (bank, n) in enumerate(plan.pt[ev]):
                            act.wait_ge(t_full[bank], n + 1)
                            nc.scalar.activation(aT_hi[:, 4 * j:4 * j + 4, :], ps_t[bank][:, :, :], ACT.Copy
                                                 ).then_inc(S["m_hi"], 1)
                        if l == 1:
                            act.wait_ge(S["m_in"], 16 * (i + 1))
                            nc.scalar.activation(aT_hi[:, 4:8, :], m[:, 512:].rearrange("p (c t) -> p c t", c=4), ACT.Copy
                                                 ).then_inc(S["m_hi"], 1)
                    elif what == 'square':
                        act.wait_ge(S["x_added"], 2 * (i + 1))
                        if i:
                            act.wait_ge(S["ms_done"], i)
                            act.wait_ge(S["sq_done"], i)
                        nc.scalar.activation(junk[:, :], x[:, :], ACT.Square, accum_out=ss[:, :]).then_inc(S["sq_done"], 1)
                    elif what == 'h':
                        act.wait_ge(S["g_full"], 2 * (i + 1))
                        for j, (bank, n) in enumerate(plan.pt[ev]):
                            act.wait_ge(t_full[bank], n + 1)
                            nc.scalar.activation(aT_hi[:, 4 * j:4 * j + 4, :], ps_t[bank][:, :, :], ACT.Copy
                                                 ).then_inc(S["h_hi"], 1)

            @block.gpsimd
            def _(pool):
                def mask_table(h, g, times):
                    pool.wait_ge(table_in[h], 32 * times)
                    t3 = table[:, h, :].rearrange("p (s c) -> p s c", s=10)
                    ins = nc.gpsimd.tensor_tensor(t3, t3, bc(cmask[:, :], 1, 10), ALU.add)
                    if g == 1:
                        ins.then_inc(S["chain"], 1)
                        pool.wait_ge(S["chain"], h + 1)
                        ins = nc.gpsimd.tensor_tensor(t3, t3, bc(rmask[:, :], 2, GRID_W), ALU.add)
                    ins.then_inc(table_ready[h], 1)

                if l == 1:
                    pool.wait_ge(S["mask_in"], 32)
                    for h in range(8):
                        mask_table(h, 0, 1)
                else:
                    nc.gpsimd.memset(zero[:, :], 0.0).then_inc(S["zero_ready"], 1)
                    pool.wait_ge(S["zero_ready"], 1)
                zeroed = 0
                for ev in plan.events:
                    what, i = ev[0], ev[1]
                    if l == 0 and what == 'probs' and i >= W_TURNS and zeroed < max_blocks(NT):
                        pool.dma_start(k.y_d[zeroed * P:(zeroed + 1) * P, :], zero[:, :]).then_inc(S["zeroed"], 16)
                        zeroed += 1
                    if what == 'out':
                        half = ev[2]
                        pool.wait_ge(S["tmp_ready"], 2 * i + half + 1)
                        pool.wait_ge(S["x_in"], 16 * (i + 1))
                        c = slice(half * 512, (half + 1) * 512)
                        nc.gpsimd.tensor_tensor(x[:, c], x[:, c], tmp[:, :], ALU.add).then_inc(S["x_added"], 1)
                    elif what == 'mean':
                        pool.wait_ge(S["ms_done"], i + 1)
                        if i:
                            pool.wait_ge(S["n_scaled"], i)
                        nc.gpsimd.tensor_tensor(rstd[:, :], ms[:, :], k.mhalf[:, 0:1], ALU.pow).then_inc(S["rstd_done"], 1)
                    elif what == 'norm':
                        pool.wait_ge(S["n_scaled"], i + 1)
                        nc.gpsimd.tensor_tensor(m[:, :], m[:, :], shift2[:, stream(i), :], ALU.add).then_inc(S["h_ready"], 1)
                    elif what == 'qk' and l == 1:
                        i, h = units[ev[1]]
                        if i and bias_group(tiles[i - 1])[0] != bias_group(tiles[i])[0]:
                            g = bias_group(tiles[i])[0]
                            mask_table(h, g, g + 1)
                if l == 0:
                    pool.wait_ge(S["zeroed"], 16 * max_blocks(NT))

            @block.vector
            def _(dve):
                dve.wait_ge(S["rows_in"], 16 * (3 * nv + 1))
                for v in range(nv):
                    nc.vector.scalar_tensor_tensor(scale2[:, v, :], scale2[:, v, :], 1.0, m[:, :], ALU.add, ALU.mult
                                                   ).then_inc(S["rows_ready"], 1)
                dve.wait_ge(S["rw_hi_done"], 1)
                nc.vector.tensor_tensor(rw_lo[:, :, :], rw[:, :, :], as_f32(rw_hi[:, :, :]), ALU.subtract).then_inc(S["rw_ready"], 1)
                for ev in plan.events:
                    what, i = ev[0], ev[1]
                    if what == 'probs' and i < W_TURNS:
                        w.rest_lo(dve, i * W_STEP, (i + 1) * W_STEP)
                    if what == 'qk':
                        u, (i, h) = i, units[i]
                        if u >= 3:
                            after_probs(dve, u - 3)
                            dve.wait_ge(S["exp_done"], u - 2)
                        for c, (bank, n, key, wd, at, biased) in enumerate(plan.chunks[u]):
                            dve.wait_ge(s_full[bank], n + 1)
                            if biased:
                                dve.wait_ge(table_ready[h], bias_group(tiles[i])[0] + 1)
                                slot = bias_slot(tiles[i]) * GRID_W
                                nc.vector.tensor_tensor_reduce(s[u % 3][:, at:at + wd], ps_s[bank][:, 0:wd],
                                                               table[:, h, slot + at:slot + at + wd], 1.0, -3.0e38, ALU.add,
                                                               ALU.max, mx[:, u % 3, c:c + 1]).then_inc(s_read[bank], 1)
                            else:
                                nc.vector.tensor_scalar(s[u % 3][:, at:at + wd], ps_s[bank][:, 0:wd], 1.0, None, ALU.mult,
                                                        ALU.max, accum_out=mx[:, u % 3, c:c + 1]).then_inc(s_read[bank], 1)
                        for bank, n, *_ in plan.chunks[u]:
                            dve.wait_ge(s_read[bank], n + 1)
                        nc.vector.tensor_reduce(nmx[:, u % 3:u % 3 + 1], mx[:, u % 3, 0:len(plan.chunks[u])], AX.X, ALU.max,
                                                negate=True).then_inc(S["max_done"], 1)
                    elif what == 'probs':
                        u = i
                        for j, (bank, n) in enumerate(plan.pt[ev]):
                            if not bank:
                                continue
                            dve.wait_ge(t_full[bank], n + 1)
                            if u >= 2:
                                dve.wait_ge(S["pv_done"], u - 1)
                            c = min(4, len(key_tiles(u)) - 4 * j)
                            nc.vector.tensor_copy(pT[u % 2][:, 4 * j:4 * j + c, :], ps_t[bank][:, 0:c, :]).then_inc(t_read[bank], 1)
                    elif what == 'q':
                        bank, n = plan.pt[ev][0]
                        dve.wait_ge(S["q_hi"], i + 1)
                        nc.vector.scalar_tensor_tensor(qT_lo[i % 2][:, :, :], ps_t[bank][:, :, :], HD ** -0.5,
                                                       as_f32(qT_hi[i % 2][:, :, :]), ALU.mult, ALU.subtract
                                                       ).then_inc(t_read[bank], 1)
                    elif what == 'heads':
                        dve.wait_ge(S["pv_done"], 8 * (i + 1))
                        dve.wait_ge(S["exp_done"], 8 * (i + 1))
                        nc.vector.reciprocal(rsums[:, :], sums[:, i % 2, :]).then_inc(S["rsum_done"], 1)
                        dve.wait_ge(S["rsum_done"], i + 1)
                        if i:
                            for bank, n in plan.pt[('h', i - 1)]:
                                dve.wait_ge(t_full[bank], n + 1)
                            dve.wait_ge(S["h_stored"], 16 * i)
                        nc.vector.tensor_tensor(m[:, 0:512].rearrange("p (h d) -> p h d", d=HD),
                                                ps_o[i % 2][:, :].rearrange("p (h d) -> p h d", d=HD), bc(rsums[:, :], 2, HD),
                                                ALU.mult).then_inc(S["heads_done"], 1)
                    elif what == 'mixed':
                        each = len(plan.pt[ev]) + (l == 1)
                        for j, (bank, n) in enumerate(plan.pt[ev]):
                            dve.wait_ge(S["m_hi"], each * i + j + 1)
                            if i:
                                dve.wait_ge(S["router_full"], i)
                            nc.vector.tensor_tensor(aT_lo[:, 4 * j:4 * j + 4, :], ps_t[bank][:, :, :],
                                                    as_f32(aT_hi[:, 4 * j:4 * j + 4, :]), ALU.subtract).then_inc(t_read[bank], 1)
                        if l == 1:
                            dve.wait_ge(S["m_hi"], each * (i + 1))
                            nc.vector.tensor_tensor(aT_lo[:, 4:8, :], m[:, 512:].rearrange("p (c t) -> p c t", c=4),
                                                    as_f32(aT_hi[:, 4:8, :]), ALU.subtract).then_inc(S["m_ready"], 1)
                    elif what == 'out':
                        half = ev[2]
                        dve.wait_ge(S["g_full"], 2 * i + half + 1)
                        if i or half:
                            dve.wait_ge(S["x_added"], 2 * i + half)
                        nc.vector.tensor_tensor(tmp[:, :], ps_g[:, :], gate[:, stream(i), half * 512:(half + 1) * 512],
                                                ALU.mult).then_inc(S["tmp_ready"], 1)
                    elif what == 'mean':
                        dve.wait_ge(S["sq_done"], i + 1)
                        if i:
                            dve.wait_ge(S["rstd_done"], i)
                        nc.vector.tensor_scalar(ms[:, :], ss[:, :], 1.0 / D, EPS, ALU.mult, ALU.add).then_inc(S["ms_done"], 1)
                    elif what == 'norm':
                        dve.wait_ge(S["rstd_done"], i + 1)
                        if l == 1:
                            dve.wait_ge(S["m_ready"], i + 1)
                        for bank, n in plan.pt[('mixed', i)]:
                            dve.wait_ge(t_full[bank], n + 1)
                        nc.vector.scalar_tensor_tensor(m[:, :], x[:, :], rstd[:, 0:1], scale2[:, stream(i), :], ALU.mult,
                                                       ALU.mult).then_inc(S["n_scaled"], 1)
                    elif what == 'h':
                        for j, (bank, n) in enumerate(plan.pt[ev]):
                            dve.wait_ge(S["h_hi"], 2 * i + j + 1)
                            dve.wait_ge(S["g_full"], 2 * (i + 1))
                            nc.vector.tensor_tensor(aT_lo[:, 4 * j:4 * j + 4, :], ps_t[bank][:, :, :],
                                                    as_f32(aT_hi[:, 4 * j:4 * j + 4, :]), ALU.subtract).then_inc(t_read[bank], 1)
                    elif what == 'router':
                        dve.wait_ge(S["router_full"], i + 1)
                        nc.vector.tensor_copy(k.logits[:, tiles[i], :], ps_g[:, 0:NE]).then_inc(S["router_done"], 1)

            @block.tensor
            def _(pe):
                def free_t(bank, n):
                    if n:
                        pe.wait_ge(t_read[bank], n)

                def split_product(out, a_hi, a_lo, b_hi, b_lo, chunks):
                    for c in range(chunks):
                        for n, (a, b) in enumerate(((a_hi, b_hi), (a_hi, b_lo), (a_lo, b_hi))):
                            mm = nc.tensor.matmul(out, a(c), b(c), start=(c == 0 and n == 0), stop=(c == chunks - 1 and n == 2))
                    return mm

                def weigh(u):
                    i, h = units[u]
                    kts = key_tiles(u)
                    if h == 0 and i >= 2:
                        pe.wait_ge(S["heads_done"], i - 1)
                    for bank, n in plan.pt[('probs', u)]:
                        pe.wait_ge(t_read[bank], n + 1)
                    for c, kt in enumerate(kts):
                        mm = nc.tensor.matmul(ps_o[i % 2][:, h * HD:(h + 1) * HD], pT[u % 2][:, c, :], values(kt, h),
                                              start=(c == 0), stop=(c == len(kts) - 1), skip_group_check=True)
                    mm.then_inc(S["pv_done"], 1)

                for ev in plan.events:
                    what, i = ev[0], ev[1]
                    if what == 'q':
                        bank, n = plan.pt[ev][0]
                        pe.wait_ge(S["q_in"], 16 * (i + 1))
                        free_t(bank, n)
                        for c in range(4):
                            mm = nc.tensor.transpose(ps_t[bank][:, c, :], q_in_sb[:, c * P:(c + 1) * P], k.ident[:, :])
                        mm.then_inc(t_full[bank], 1)
                    elif what == 'qk':
                        u, (i, h) = i, units[i]
                        if h == 0:
                            bank, n = plan.pt[('q', i)][0]
                            pe.wait_ge(t_read[bank], n + 1)
                        for bank, n, key, wd, at, _b in plan.chunks[u]:
                            if n:
                                pe.wait_ge(s_read[bank], n)
                            for j, (a, b) in enumerate(((0, 0), (0, 1), (1, 0))):
                                mm = nc.tensor.matmul(ps_s[bank][:, 0:wd], qT(a, i, h), kT(b, h, key, wd), start=(j == 0),
                                                      stop=(j == 2))
                            mm.then_inc(s_full[bank], 1)
                    elif what == 'probs':
                        u = i
                        kts = key_tiles(u)
                        pe.wait_ge(S["exp_done"], u + 1)
                        last = min(2, len(plan.pt[ev]) - 1)
                        for j, (bank, n) in enumerate(plan.pt[ev]):
                            if u and j == last:
                                weigh(u - 1)
                            free_t(bank, n)
                            for c in range(min(4, len(kts) - 4 * j)):
                                mm = nc.tensor.transpose(ps_t[bank][:, c, :], s[u % 3][:, (4 * j + c) * P:(4 * j + c + 1) * P],
                                                         k.ident[:, :])
                            mm.then_inc(t_full[bank], 1)
                    elif what == 'pv' and i == len(units) - 1:
                        weigh(i)
                    elif what == 'mixed':
                        pe.wait_ge(S["heads_done"], i + 1)
                        if l == 0:
                            pe.wait_ge(S["m_in"], 16 * (i + 1))
                        for j, (bank, n) in enumerate(plan.pt[ev]):
                            free_t(bank, n)
                            for c in range(4):
                                mm = nc.tensor.transpose(ps_t[bank][:, c, :], m[:, (4 * j + c) * P:(4 * j + c + 1) * P],
                                                         k.ident[:, :])
                            mm.then_inc(t_full[bank], 1)
                    elif what == 'out':
                        half = ev[2]
                        if i == 0 and half == 0:
                            w.wait_all(pe)
                        for bank, n in plan.pt[('mixed', i)]:
                            pe.wait_ge(t_read[bank], n + 1)
                        if l == 1:
                            pe.wait_ge(S["m_ready"], i + 1)
                        if i or half:
                            pe.wait_ge(S["tmp_ready"], 2 * i + half)
                        if i and not half:
                            pe.wait_ge(S["router_done"], i)
                        split_product(ps_g[:, :], lambda c: aT_hi[:, c, :], lambda c: aT_lo[:, c, :],
                                      lambda c: w.hi[:, c, half * 512:(half + 1) * 512],
                                      lambda c: w.lo[:, c, half * 512:(half + 1) * 512], KD).then_inc(S["g_full"], 1)
                    elif what == 'h':
                        pe.wait_ge(S["h_ready"], i + 1)
                        for j, (bank, n) in enumerate(plan.pt[ev]):
                            free_t(bank, n)
                            for c in range(4):
                                mm = nc.tensor.transpose(ps_t[bank][:, c, :], m[:, (4 * j + c) * P:(4 * j + c + 1) * P],
                                                         k.ident[:, :])
                            mm.then_inc(t_full[bank], 1)
                    elif what == 'router':
                        if i == 0:
                            pe.wait_ge(S["rw_ready"], 1)
                        for bank, n in plan.pt[('h', i)]:
                            pe.wait_ge(t_read[bank], n + 1)
                        pe.wait_ge(S["tmp_ready"], 2 * (i + 1))
                        split_product(ps_g[:, 0:NE], lambda c: aT_hi[:, c, :], lambda c: aT_lo[:, c, :],
                                      lambda c: rw_hi[:, c, :], lambda c: rw_lo[:, c, :], KD).then_inc(S["router_full"], 1)


def bias_slot(tile):
    first = key_plan(1, tile)[0][0]
    return 2 * (first - tile) + 7 - bias_group(tile)[1]


def moe(nc, k, keep, l, t, nt):
    k.dest = keep.enter_context(nc.sbuf_tensor(f"dest{l}", [P, 2, NT], I32))
    k.weight = keep.enter_context(nc.sbuf_tensor(f"weight{l}", [P, 2, NT], F32))
    k.blocks = keep.enter_context(nc.sbuf_tensor(f"blocks{l}", [P, 3, NE], I32))
    with Phase(nc, f"mw{l}") as ph:
        raw = RawWeights(ph, t['moe_w_gate'][l], t['moe_w_up'][l], t['moe_w_down'][l])
        route(nc, k, l, nt, raw, t['k_lower'], t['k_count'], t['k_token'])
        experts(nc, k, l, raw, nt)


class RawWeights:

    def __init__(self, ph, w_gate, w_up, w_down):
        self.gate, self.up, self.down = w_gate, w_up, w_down
        self.gu = [ph.sb(f"gu{p}", [P, KD, 2 * F]) for p in range(2)]
        self.d = ph.sb("d", [P, KF, D])
        self.gu_in, self.d_in = [ph.sem(f"gu_in{p}") for p in range(2)], ph.sem("d_in")

    def load_gu(self, sp, e, p):
        for j, w in enumerate((self.gate, self.up)):
            sp.dma_start(self.gu[p][:, :, j * F:(j + 1) * F], w[bass.ds(e, 1)].rearrange("o (c p) f -> p (o c) f", p=P)
                         ).then_inc(self.gu_in[p], 16)

    def load_d(self, sp, e):
        sp.dma_start(self.d[:, :, :], self.down[bass.ds(e, 1)].rearrange("o (c p) f -> p (o c) f", p=P)
                     ).then_inc(self.d_in, 16)


def route(nc, k, l, nt, raw, lower, count, token):
    with Phase(nc, f"ro{l}") as ph:
        aff, sel = ph.sb("aff", [P, nt, NE]), ph.sb("sel", [P, nt, NE])
        bias = ph.sb("bias", [P, NE])
        low = ph.sb("low", [P, P])
        ones = ph.sb("ones", [P, P])
        cnt_c = ph.sb("cnt_c", [P, 2 * NE])
        tok = ph.sb("tok", [P, NT], I32)
        zero = ph.sb("zero", [P, max_blocks(nt) + 1], I32)
        pair = ph.sb("pair", [P, 2, nt * NGRP, 2])
        two = ph.sb("two", [P, 3, nt * NGRP])
        best = ph.sb("best", [P, 2, nt])
        gmask = ph.sb("gmask", [P, nt, NGRP])
        cand = ph.sb("cand", [P, nt, NE])
        one = [ph.sb(f"one{j}", [P, nt, NE]) for j in range(2)]
        both = ph.sb("both", [P, nt, NE])
        before = ph.sb("before", [P, nt, NE])
        run = ph.sb("run", [P, NE])
        over = ph.sb("over", [P, NE, nt - 1])
        nb = ph.sb("nb", [P, NE])
        cum = [ph.sb(f"cum{j}", [P, NE]) for j in range(2)]
        wsum = ph.sb("wsum", [P, nt])
        dest = ph.sb("dest", [P, 2, nt])
        ps_before, ps_total = ph.ps("ps_before", [P, nt * NE]), ph.ps("ps_total", [P, nt * NE])
        consts_in, bias_in, aff_done, chain_v = ph.sem("consts_in"), ph.sem("bias_in"), ph.sem("aff_done"), ph.sem("chain_v")
        both_ready, sums_full, dest_ready = ph.sem("both_ready"), ph.sem("sums_full"), ph.sem("dest_ready")
        zero_ready, zeroed, scattered = ph.sem("zero_ready"), ph.sem("zeroed"), ph.sem("scattered")
        ones_ready = ph.sem("ones_ready")
        with nc.Block() as block:

            @block.sync
            def _(sp):
                sp.dma_start(bias[:, :], k.router_b.partition_broadcast(P)).then_inc(consts_in, 16)
                sp.dma_start(low[:, :], lower).then_inc(consts_in, 16)
                sp.dma_start(cnt_c[:, :], count).then_inc(consts_in, 16)
                sp.dma_start(tok[:, :], token).then_inc(consts_in, 16)
                raw.load_gu(sp, 0, 0)
                raw.load_d(sp, 0)
                raw.load_gu(sp, 1, 1)
                sp.wait_ge(consts_in, 64)

            @block.scalar
            def _(act):
                nc.scalar.activation(aff[:, :, :], k.logits[:, 0:nt, :], ACT.Sigmoid).then_inc(aff_done, 1)

            @block.vector
            def _(dve):
                step = chain(dve, chain_v)
                tt, ts, red = nc.vector.tensor_tensor, nc.vector.tensor_scalar, nc.vector.tensor_reduce
                dve.wait_ge(consts_in, 64)
                dve.wait_ge(aff_done, 1)
                step(tt(sel[:, :, :], aff[:, :, :], bc(bias[:, :], 1, nt), ALU.add))
                s4 = sel[:, :, :].rearrange("p t (g a b) -> p (t g) a b", g=NGRP, a=2)
                step(tt(pair[:, 0], s4[:, :, :, 0], s4[:, :, :, 1], ALU.max))
                step(tt(pair[:, 1], s4[:, :, :, 0], s4[:, :, :, 1], ALU.min))
                step(tt(two[:, 0], pair[:, 0, :, 0], pair[:, 0, :, 1], ALU.max))
                step(tt(two[:, 1], pair[:, 0, :, 0], pair[:, 0, :, 1], ALU.min))
                step(tt(two[:, 2], pair[:, 1, :, 0], pair[:, 1, :, 1], ALU.max))
                step(tt(two[:, 1], two[:, 1], two[:, 2], ALU.max))
                step(tt(two[:, 0], two[:, 0], two[:, 1], ALU.add))

                def first_best(score, n, out):
                    step(red(best[:, 0], score, AX.X, ALU.max))
                    c = cand[:, :, 0:n]
                    step(tt(c, score, bc(best[:, 0], 2, n), ALU.is_equal))
                    step(ts(c, c, -100.0, 100.0, ALU.mult, ALU.add))
                    step(tt(c, c, bc(cnt_c[:, 0:n], 1, nt), ALU.add))
                    step(red(best[:, 1], c, AX.X, ALU.min))
                    step(tt(out, bc(best[:, 1], 2, n), bc(cnt_c[:, 0:n], 1, nt), ALU.is_equal))

                first_best(two[:, 0].rearrange("p (t g) -> p t g", t=nt), NGRP, gmask[:, :, :])
                step(ts(gmask[:, :, :], gmask[:, :, :], BIG, -BIG, ALU.mult, ALU.add))
                g4 = gmask[:, :, :].rearrange("p t g -> p (t g)")
                s3 = sel[:, :, :].rearrange("p t (g e) -> p (t g) e", g=NGRP)
                step(tt(s3, s3, bc(g4, 2, EPG), ALU.add))
                first_best(sel[:, :, :], NE, one[0][:, :, :])
                o2, s2 = (a[:, :, :].rearrange("p t e -> p (t e)") for a in (one[0], sel))
                step(nc.vector.scalar_tensor_tensor(s2, o2, -2.0 * BIG, s2, ALU.mult, ALU.add))
                first_best(sel[:, :, :], NE, one[1][:, :, :])
                tt(both[:, :, :], one[0][:, :, :], one[1][:, :, :], ALU.add).then_inc(both_ready, 1)
                for j in range(2):
                    step(tt(cand[:, :, :], aff[:, :, :], one[j][:, :, :], ALU.mult))
                    step(red(k.weight[:, j, 0:nt], cand[:, :, :], AX.X, ALU.add))
                step(tt(wsum[:, :], k.weight[:, 0, 0:nt], k.weight[:, 1, 0:nt], ALU.add))
                step(nc.vector.reciprocal(wsum[:, :], wsum[:, :]))
                for j in range(2):
                    step(tt(k.weight[:, j, 0:nt], k.weight[:, j, 0:nt], wsum[:, :], ALU.mult))
                dve.wait_ge(sums_full, 1)
                step(nc.vector.tensor_copy(before[:, :, :].rearrange("p t e -> p (t e)"), ps_before[:, :]))
                step(nc.vector.tensor_copy(run[:, :], ps_total[:, 0:NE]))
                for i in range(1, nt):
                    step(tt(before[:, i, :], before[:, i, :], run[:, :], ALU.add))
                    step(tt(run[:, :], run[:, :], ps_total[:, i * NE:(i + 1) * NE], ALU.add))
                step(tt(over[:, :, :], bc(run[:, :], 2, nt - 1), bc(cnt_c[:, NE:NE + nt - 1], 1, NE), ALU.is_gt))
                step(red(nb[:, :], over[:, :, :], AX.X, ALU.add))
                step(ts(nb[:, :], nb[:, :], 1.0, None, ALU.add))
                step(nc.vector.tensor_copy(cum[0][:, :], nb[:, :]))
                for j, d in enumerate((1, 2, 4, 8)):
                    a, b = cum[j % 2], cum[1 - j % 2]
                    step(nc.vector.tensor_copy(b[:, 0:d], a[:, 0:d]))
                    step(tt(b[:, d:NE], a[:, d:NE], a[:, 0:NE - d], ALU.add))
                step(tt(cum[0][:, :], cum[0][:, :], nb[:, :], ALU.subtract))
                step(nc.vector.tensor_copy(k.blocks[:, 0, :], nb[:, :]))
                step(ts(cum[1][:, :], cum[0][:, :], -1.0, 0.0, ALU.add, ALU.max))
                step(nc.vector.tensor_copy(k.blocks[:, 1, :], cum[1][:, :]))
                step(tt(nb[:, :], cum[0][:, :], nb[:, :], ALU.add))
                step(nc.vector.tensor_copy(k.blocks[:, 2, :], nb[:, :]))
                step(ts(cum[1][:, :], cum[0][:, :], float(P), None, ALU.mult))
                step(tt(before[:, :, :], before[:, :, :], bc(cum[1][:, :], 1, nt), ALU.add))
                for j in range(2):
                    step(tt(cand[:, :, :], before[:, :, :], one[j][:, :, :], ALU.mult))
                    step(red(dest[:, j], cand[:, :, :], AX.X, ALU.add))
                nc.vector.tensor_copy(k.dest[:, :, 0:nt], dest[:, :, :]).then_inc(dest_ready, 1)

            @block.tensor
            def _(pe):
                pe.wait_ge(both_ready, 1)
                pe.wait_ge(ones_ready, 1)
                b = both[:, :, :].rearrange("p t e -> p (t e)")
                nc.tensor.matmul(ps_before[:, :], low[:, :], b, start=True, stop=True)
                nc.tensor.matmul(ps_total[:, :], ones[:, :], b, start=True, stop=True).then_inc(sums_full, 1)

            @block.gpsimd
            def _(pool):
                nc.gpsimd.memset(ones[:, :], 1.0).then_inc(ones_ready, 1)
                nc.gpsimd.memset(zero[:, :], 0).then_inc(zero_ready, 1)
                pool.wait_ge(zero_ready, 1)
                pool.dma_start(k.slot_d[l].rearrange("(p c) o -> p (c o)", p=P), zero[:, :]).then_inc(zeroed, 16)
                pool.wait_ge(zeroed, 16)
                pool.wait_ge(dest_ready, 1)
                for j in range(2):
                    for i in range(nt):
                        pool.indirect_dma_start(k.slot_d[l], bass.IndirectOffsetOnAxis(k.dest[:, j, i:i + 1], 0),
                                                tok[:, i:i + 1], None).then_inc(scattered, 16)
                pool.wait_ge(scattered, 16 * 2 * nt)


def experts(nc, k, l, raw, nt):
    most = max_blocks(nt)
    with Phase(nc, f"ex{l}") as ph:
        gu_hi, gu_lo = ph.sb("gu_hi", [P, KD, 2 * F], F32R), ph.sb("gu_lo", [P, KD, 2 * F], F32R)
        d_hi, d_lo = ph.sb("d_hi", [P, KF, D], F32R), ph.sb("d_lo", [P, KF, D], F32R)
        slot_rows, slot_f = ph.sb("slot_rows", [most + 1, P], I32), ph.sb("slot_f", [most + 1, P])
        slots = ph.sb("slots", [P, most + 1], I32)
        at, nil = (ph.sb(x, [P, 1], I32) for x in ("at", "nil"))
        x = ph.sb("x", [P, D])
        xT_hi, xT_lo = ph.sb("xT_hi", [P, KD, P], F32R), ph.sb("xT_lo", [P, KD, P], F32R)
        sg = ph.sb("sg", [P, F])
        h = sg
        hT_hi, hT_lo = ph.sb("hT_hi", [P, KF, P], F32R), ph.sb("hT_lo", [P, KF, P], F32R)
        y = ph.sb("y", [P, D])
        ps_x = [ph.ps(f"ps_x{i}", [P, 4, P]) for i in range(2)]
        ps_g, ps_u, ps_h = ph.ps("ps_g", [P, F]), ph.ps("ps_u", [P, F]), ph.ps("ps_h", [P, KF, P])
        ps_y = [ph.ps(f"ps_y{i}", [P, 512]) for i in range(2)]
        S = {n: ph.sem(n) for n in "slots_in slots_float slots_full slots_ready at_ready x_in g_full gu_full silu_done h_ready h_full h_hi h_lo x_hi gu_hi_done gu_ready d_hi_done d_ready y_out".split()}
        x_full = [ph.sem(f"x_full{i}") for i in range(2)]
        x_read = [ph.sem(f"x_read{i}") for i in range(2)]
        y_full = [ph.sem(f"y_full{i}") for i in range(2)]
        y_read = [ph.sem(f"y_read{i}") for i in range(2)]
        PIECES = 4

        def piece(j):
            return slice((j % 2) * 4, (j % 2) * 4 + 4), slice((j // 2) * F, (j // 2 + 1) * F)

        def block_range(eng, e):
            n = eng.value_load(k.blocks[0:1, 0, bass.ds(e, 1)], min_val=1, max_val=nt)
            if isinstance(e, int) and e == 0:
                return n, 0
            return n, eng.value_load(k.blocks[0:1, 1, bass.ds(e, 1)], min_val=0, max_val=most) + 1

        def within(n, top):
            return n if isinstance(n, int) else nc.s_assert_within(n, 0, top, skip_runtime_bounds_check_because="all blocks together are at most that many")

        def for_experts(eng, one):
            one(0, 0, 0)
            with eng.Fori(0, (NE - 2) // 2) as g:
                one(2 * g + 1, 1, g)
                one(2 * g + 2, 0, g + 1)
            one(NE - 1, 1, NE // 2 - 1)

        def per_block(eng, e, turn):
            count, first = block_range(eng, e)
            turn(first, True, lambda: eng.If(count < 2))
            with eng.If(count > 1):
                with eng.Fori(1, count) as b:
                    turn(first + b, False, lambda: eng.If(b + 1 >= count))
            return first + count

        with nc.Block() as block:

            @block.sync
            def _(sp):
                sp.dma_start(slot_rows[:, :], k.slot_d[l].rearrange("(b p) o -> b (p o)", p=P)).then_inc(S["slots_in"], 16)

                def one(e, p):
                    sp.wait_ge(S["gu_ready"], PIECES * (e + 1))
                    raw.load_gu(sp, e + 2, p)
                    sp.wait_ge(S["d_ready"], 2 * (e + 1))
                    raw.load_d(sp, e + 1)

                with sp.Fori(0, (NE - 2) // 2) as g:
                    one(2 * g, 0)
                    one(2 * g + 1, 1)
                sp.wait_ge(S["d_ready"], 2 * (NE - 1))
                raw.load_d(sp, NE - 1)

            @block.gpsimd
            def _(pool):
                def fetch(n, first=False):
                    if not first:
                        pool.wait_ge(S["x_in"], 16 * n)
                        for i in range(2):
                            pool.wait_ge(x_full[i], n)
                    nc.gpsimd.tensor_tensor(at[:, :], slots[:, bass.ds(within(n, most), 1)], nil[:, :], ALU.add
                                            ).then_inc(S["at_ready"], 1)
                    pool.wait_ge(S["at_ready"], 1)
                    pool.sem_clear(S["at_ready"])
                    pool.indirect_dma_start(x[:, :], None, k.h_d, bass.IndirectOffsetOnAxis(at[:, 0:1], 0)
                                            ).then_inc(S["x_in"], 16)

                nc.gpsimd.memset(y[:, 0:512], 0.0).then_inc(y_read[0], 1)
                nc.gpsimd.memset(nil[:, :], 0).then_inc(S["at_ready"], 1)
                pool.wait_ge(S["at_ready"], 1)
                pool.sem_clear(S["at_ready"])
                pool.wait_ge(S["slots_ready"], 1)
                fetch(0, True)
                count = [None]

                def one(e, p, n):
                    count[0] = per_block(pool, e, lambda n, head, at_last: fetch(n + 1))

                for_experts(pool, one)
                pool.wait_ge(S["x_in"], 16 * count[0] + 16)
                pool.wait_ge(S["y_out"], 16 * count[0] + 16)

            @block.scalar
            def _(act):
                def copy(dst, src, sem):
                    nc.scalar.activation(dst, src, ACT.Copy).then_inc(sem, 1)

                def split_gu(p, n, half):
                    act.wait_ge(raw.gu_in[p], 32 * n + 32)
                    for j in (2 * half, 2 * half + 1):
                        c, f = piece(j)
                        copy(gu_hi[:, c, f], raw.gu[p][:, c, f], S["gu_hi_done"])

                def split_d(e):
                    act.wait_ge(raw.d_in, 16 * e + 16)
                    for j in range(2):
                        copy(d_hi[:, 2 * j:2 * j + 2, :], raw.d[:, 2 * j:2 * j + 2, :], S["d_hi_done"])

                def split_x(n, first=False):
                    if not first:
                        act.wait_ge(S["gu_full"], n)
                    for i in range(2):
                        act.wait_ge(x_full[i], n + 1)
                        copy(xT_hi[:, 4 * i:4 * i + 4, :], ps_x[i][:, :, :], S["x_hi"])

                def lowered(n):
                    act.wait_ge(y_full[0], n + 1)
                    act.wait_ge(S["y_out"], 16 * n + 16)
                    copy(y[:, 0:512], ps_y[0][:, :], y_read[0])

                def store(n):
                    for i in range(2):
                        act.wait_ge(y_read[i], n + 2)
                    act.dma_start(k.y_d.rearrange("(b p) d -> b p d", p=P)[bass.ds(within(n, most - 1), 1)].rearrange("b p d -> (b p) d"),
                                  y[:, :]).then_inc(S["y_out"], 16)

                def one(e, p, n_used):
                    last_expert = isinstance(e, int) and e == NE - 1

                    def turn(n, head, at_last):
                        start = isinstance(n, int)
                        act.wait_ge(S["g_full"], n + 1)
                        if not start:
                            act.wait_ge(S["h_full"], n)
                        nc.scalar.activation(sg[:, :], ps_g[:, :], ACT.Silu).then_inc(S["silu_done"], 1)
                        if not last_expert:
                            with at_last():
                                split_gu(1 - p, n_used + p, 0)
                        split_x(n + 1)
                        if not last_expert:
                            with at_last():
                                split_gu(1 - p, n_used + p, 1)
                        if not start:
                            lowered(n - 1)
                        act.wait_ge(S["h_full"], n + 1)
                        if not start:
                            act.wait_ge(y_full[1], n)
                        copy(hT_hi[:, :, :], ps_h[:, :, :], S["h_hi"])
                        if not start:
                            store(n - 1)
                        if head:
                            split_d(e)
                    return per_block(act, e, turn)

                for i in range(2):
                    act.wait_ge(y_read[i], 1)
                act.dma_start(k.spare_d, y[0:1, :]).then_inc(S["y_out"], 16)
                split_gu(0, 0, 0)
                split_gu(0, 0, 1)
                split_x(0, True)
                total = [None]

                def keep(e, p, n):
                    total[0] = one(e, p, n)

                for_experts(act, keep)
                lowered(total[0] - 1)
                store(total[0] - 1)

            @block.vector
            def _(dve):
                sub = lambda dst, a, b, sem: nc.vector.tensor_tensor(dst, a, as_f32(b), ALU.subtract).then_inc(sem, 1)

                def split_gu(e, p, half):
                    for j in (2 * half, 2 * half + 1):
                        c, f = piece(j)
                        dve.wait_ge(S["gu_hi_done"], PIECES * e + j + 1)
                        sub(gu_lo[:, c, f], raw.gu[p][:, c, f], gu_hi[:, c, f], S["gu_ready"])

                def split_d(e):
                    for j in range(2):
                        c = slice(2 * j, 2 * j + 2)
                        dve.wait_ge(S["d_hi_done"], 2 * e + j + 1)
                        sub(d_lo[:, c, :], raw.d[:, c, :], d_hi[:, c, :], S["d_ready"])

                def split_x(n):
                    for i in range(2):
                        dve.wait_ge(S["x_hi"], 2 * n + i + 1)
                        sub(xT_lo[:, 4 * i:4 * i + 4, :], ps_x[i][:, :, :], xT_hi[:, 4 * i:4 * i + 4, :], x_read[i])

                def lowered(n):
                    dve.wait_ge(y_full[1], n + 1)
                    dve.wait_ge(S["y_out"], 16 * n + 16)
                    nc.vector.tensor_copy(y[:, 512:], ps_y[1][:, :]).then_inc(y_read[1], 1)

                def one(e, p, n_used):
                    last_expert = isinstance(e, int) and e == NE - 1

                    def turn(n, head, at_last):
                        start = isinstance(n, int)
                        if not last_expert:
                            with at_last():
                                split_gu(e + 1, 1 - p, 0)
                        dve.wait_ge(S["gu_full"], n + 1)
                        dve.wait_ge(S["silu_done"], n + 1)
                        nc.vector.tensor_tensor(h[:, :], sg[:, :], ps_u[:, :], ALU.mult).then_inc(S["h_ready"], 1)
                        split_x(n + 1)
                        if not last_expert:
                            with at_last():
                                split_gu(e + 1, 1 - p, 1)
                        if not start:
                            lowered(n - 1)
                        dve.wait_ge(S["h_hi"], n + 1)
                        sub(hT_lo[:, :, :], ps_h[:, :, :], hT_hi[:, :, :], S["h_lo"])
                        if head:
                            split_d(e)
                    return per_block(dve, e, turn)

                nc.vector.memset(y[:, 512:], 0.0).then_inc(y_read[1], 1)
                dve.wait_ge(S["slots_in"], 16)
                nc.vector.tensor_copy(slot_f[:, :], slot_rows[:, :]).then_inc(S["slots_float"], 1)
                dve.wait_ge(S["slots_full"], 1)
                nc.vector.tensor_copy(slots[:, :], ps_g[:, 0:most + 1]).then_inc(S["slots_ready"], 1)
                split_gu(0, 0, 0)
                split_gu(0, 0, 1)
                split_x(0)
                total = [None]

                def keep(e, p, n):
                    total[0] = one(e, p, n)

                for_experts(dve, keep)
                lowered(total[0] - 1)

            @block.tensor
            def _(pe):
                def transpose_x(n, first=False):
                    pe.wait_ge(S["x_in"], 16 * n + 16)
                    for i in range(2):
                        if not first:
                            pe.wait_ge(x_read[i], n)
                        for q in range(4):
                            c = 4 * i + q
                            mm = nc.tensor.transpose(ps_x[i][:, q, :], x[:, c * P:(c + 1) * P], k.ident[:, :])
                        mm.then_inc(x_full[i], 1)

                def product(out, a_hi, a_lo, b_hi, b_lo, chunks, cols):
                    for c in range(chunks):
                        for j, (a, b) in enumerate(((a_hi, b_hi), (a_hi, b_lo), (a_lo, b_hi))):
                            mm = nc.tensor.matmul(out, a[:, c, :], b[:, c, cols], start=(c == 0 and j == 0),
                                                  stop=(c == chunks - 1 and j == 2))
                    return mm

                def lower(n, e):
                    pe.wait_ge(S["d_ready"], 2 * e + 2)
                    pe.wait_ge(S["h_lo"], n + 1)
                    for i in range(2):
                        pe.wait_ge(y_read[i], n + 1)
                        product(ps_y[i][:, :], hT_hi, hT_lo, d_hi, d_lo, KF, slice(i * 512, i * 512 + 512)
                                ).then_inc(y_full[i], 1)

                def one(e, p, n_used):
                    def turn(n, head, at_last):
                        start = isinstance(n, int)
                        if head:
                            pe.wait_ge(S["gu_ready"], PIECES * e + 2)
                        for i in range(2):
                            pe.wait_ge(x_read[i], n + 1)
                        if not start:
                            pe.wait_ge(S["h_ready"], n)
                        product(ps_g[:, :], xT_hi, xT_lo, gu_hi, gu_lo, KD, slice(0, F)).then_inc(S["g_full"], 1)
                        if head:
                            pe.wait_ge(S["gu_ready"], PIECES * e + PIECES)
                        product(ps_u[:, :], xT_hi, xT_lo, gu_hi, gu_lo, KD, slice(F, 2 * F)).then_inc(S["gu_full"], 1)
                        transpose_x(n + 1)
                        if not start:
                            lower(n - 1, e - 1 if head else e)
                        pe.wait_ge(S["h_ready"], n + 1)
                        if not start:
                            pe.wait_ge(S["h_lo"], n)
                        for c in range(KF):
                            mm = nc.tensor.transpose(ps_h[:, c, :], h[:, c * P:(c + 1) * P], k.ident[:, :])
                        mm.then_inc(S["h_full"], 1)
                    return per_block(pe, e, turn)

                pe.wait_ge(S["slots_float"], 1)
                nc.tensor.transpose(ps_g[:, 0:most + 1], slot_f[:, :], k.ident[0:most + 1, 0:most + 1]).then_inc(S["slots_full"], 1)
                pe.wait_ge(S["slots_ready"], 1)
                transpose_x(0, True)
                total = [None]

                def keep(e, p, n):
                    total[0] = one(e, p, n)

                for_experts(pe, keep)
                lower(total[0] - 1, NE - 1)


def combine(nc, k, l, nt, w=None):
    last = nt == LT
    with Phase(nc, f"co{l}") as ph:
        nv = 1 if last else 2
        gate = ph.sb("gate", [P, nv, D])
        x = [ph.sb(f"x{p}", [P, D]) for p in range(2)]
        y = [[ph.sb(f"y{j}{p}", [P, D]) for p in range(2)] for j in range(2)]
        gate_in, chain_v = ph.sem("gate_in"), ph.sem("chain_v")
        x_in = [ph.sem(f"x_in{p}") for p in range(2)]
        y_in = [[ph.sem(f"y_in{j}{p}") for p in range(2)] for j in range(2)]
        out = [ph.sem(f"out{p}") for p in range(2)]
        done = ph.sem("done")
        with nc.Block() as block:

            @block.sync
            def _(sp):
                for v in range(nv):
                    sp.dma_start(gate[:, v, :], k.mod_d[l, v, G2 * D:(G2 + 1) * D].partition_broadcast(P)).then_inc(gate_in, 16)
                for i in range(nt + 2):
                    if i < nt:
                        if i >= 2:
                            sp.wait_ge(out[i % 2], 16 * (i // 2))
                        sp.dma_start(x[i % 2][:, :], k.x_d[i * P:(i + 1) * P, :]).then_inc(x_in[i % 2], 16)
                    if i:
                        j = i - 1
                        if j < nt:
                            sp.wait_ge(done, j + 1)
                            dst = k.out[0, j * P:(j + 1) * P, :] if last else k.x_d[j * P:(j + 1) * P, :]
                            sp.dma_start(dst, x[j % 2][:, :]).then_inc(out[j % 2], 16)
                for p in range(2):
                    sp.wait_ge(out[p], 16 * (nt // 2))

            @block.scalar
            def _(act):
                if w is not None:
                    for i in range(len(w.pieces)):
                        w.load(act, i, i + 1)
                        if i:
                            w.round_hi(act, i - 1, i)
                    w.round_hi(act, len(w.pieces) - 1)

            @block.gpsimd
            def _(pool):
                for i in range(nt):
                    for j in range(2):
                        if i >= 2:
                            pool.wait_ge(done, i - 1)
                        pool.indirect_dma_start(y[j][i % 2][:, :], None, k.y_d,
                                                bass.IndirectOffsetOnAxis(k.dest[:, j, i:i + 1], 0)).then_inc(y_in[j][i % 2], 16)

            @block.vector
            def _(dve):
                step = chain(dve, chain_v)
                dve.wait_ge(gate_in, 16 * nv)
                for i in range(nt):
                    p, v = i % 2, 1 if i >= LT else 0
                    a, b = y[0][p][:, :], y[1][p][:, :]
                    dve.wait_ge(y_in[0][p], 16 * (i // 2 + 1))
                    step(nc.vector.tensor_scalar(a, a, k.weight[:, 0, i:i + 1], None, ALU.mult))
                    dve.wait_ge(y_in[1][p], 16 * (i // 2 + 1))
                    step(nc.vector.scalar_tensor_tensor(b, b, k.weight[:, 1, i:i + 1], a, ALU.mult, ALU.add))
                    step(nc.vector.tensor_tensor(b, b, gate[:, v, :], ALU.mult))
                    dve.wait_ge(x_in[p], 16 * (i // 2 + 1))
                    nc.vector.tensor_tensor(x[p][:, :], x[p][:, :], b, ALU.add).then_inc(done, 1)
                    if w is not None and 2 * i < len(w.pieces):
                        w.rest_lo(dve, 2 * i, 2 * i + 2)


_INS = ['x', 'c', 'ctx', 'c_ctx', 'router_w', 'router_b', 'ada_w', 'ada_b', 'norm1_g', 'norm2_g',
        'ev_w_in', 'ev_w_out', 'a_q_norm', 'a_k_norm', 'b_v_norm', 'b_ws', 'b_bs',
        'od_w_in', 'od_w_out', 'c_q_norm', 'c_k_norm', 'c_rpb', 'd_dw', 'd_dw_b', 'd_ln_g', 'd_ln_b',
        'moe_w_gate', 'moe_w_up', 'moe_w_down']


def constants():
    t = np.arange(SEQ)
    freq = 10000.0 ** (-np.arange(HD // 4, dtype=np.float32) / np.float32(HD // 4))
    pos = np.stack([t // GRID_W, t % GRID_W], -1).astype(np.float32)
    ang = pos[:, :, None] * freq.astype(np.float32)
    cos = np.repeat(np.cos(ang)[:, :, None, :], 2, 2).reshape(SEQ, HD)
    sin = (np.sin(ang)[:, :, None, :] * np.array([-1.0, 1.0], np.float32)[None, None, :, None]).reshape(SEQ, HD)
    rope = np.zeros((NT * P, 2, HD), np.float32)
    rope[:, 0] = 1.0
    rope[:SEQ, 0], rope[:SEQ, 1] = cos, sin
    rope = np.ascontiguousarray(rope.reshape(NT, P, 2, HD).transpose(1, 0, 2, 3))
    col = np.arange(GRID_W)
    first = np.clip(col - 8, 0, GRID_W - 16)
    seen = (col[None, :] >= first[:, None]) & (col[None, :] < first[:, None] + 16)
    colmask = np.tile(np.where(seen, 0.0, -BIG).astype(np.float32), (2, 1))
    half = np.arange(P)[:, None] // GRID_W
    slot = np.arange(10)[None, :]
    rowmask = np.where((slot >= half) & (slot < half + WIN_ROWS), 0.0, -BIG).astype(np.float32)
    token = np.arange(NT * P, dtype=np.int32).reshape(NT, P).T
    count = np.tile(np.concatenate([np.arange(NE), P * (1 + np.arange(NE))]).astype(np.float32), (P, 1))
    lower = (np.arange(P)[:, None] < np.arange(P)[None, :]).astype(np.float32)
    return {'k_token': np.ascontiguousarray(token), 'k_count': count, 'k_lower': lower,
            'k_ident': np.eye(P, dtype=np.float32), 'k_rope': rope, 'k_colmask': colmask, 'k_rowmask': rowmask}


def build(nc, t, out, stop=None):
    k = Kit()
    k.norm1_g, k.norm2_g, k.router_w, k.router_b = t['norm1_g'], t['norm2_g'], t['router_w'], t['router_b']

    def dram(name, shape, dt=F32):
        return nc.dram_tensor(name, shape, dt).ap()

    k.mod_d = dram("mod_d", [2, 2, MOD])
    k.q_d = dram("q_d", [NT * P, A_Q])
    k.m_d = dram("m_d", [NT * P, BW])
    k.mT_d = dram("mT_d", [BW, SEQ])
    k.x_d = dram("x_d", [NT * P, D])
    k.h_d = dram("h_d", [NT * P, D])
    k.y_d = dram("y_d", [max_blocks(NT) * P, D])
    k.spare_d = dram("spare_d", [1, D])
    k.slot_d = [dram(f"slot_d{l}", [(max_blocks(n) + 1) * P, 1], I32) for l, n in enumerate((NT, LT))]
    k.rpb_d = dram("rpb_d", [8, 15, GRID_W, P])
    k.out = out

    def stream_in(tile):
        return t['x'][0, tile * P:(tile + 1) * P, :] if tile < LT else t['ctx'][0, (tile - LT) * P:(tile - LT + 1) * P, :]

    def stream_mid(tile):
        return k.x_d[tile * P:(tile + 1) * P, :]

    k.stream_in, k.stream_mid = stream_in, stream_mid
    with ExitStack() as ctx:
        k.ident = ctx.enter_context(nc.sbuf_tensor("ident", [P, P], F32))
        k.mhalf = ctx.enter_context(nc.sbuf_tensor("mhalf", [P, 1], F32))
        k.logits = ctx.enter_context(nc.sbuf_tensor("logits", [P, NT, NE], F32))
        const_in = ctx.enter_context(nc.semaphore("const_in"))
        with nc.Block() as block:

            @block.sync
            def _(sp):
                sp.dma_start(k.ident[:, :], t['k_ident']).then_inc(const_in, 16)
                sp.wait_ge(const_in, 16)

            @block.gpsimd
            def _(pool):
                nc.gpsimd.memset(k.mhalf[:, :], -0.5)

        modulation(nc, k, t['c'], t['c_ctx'], t['ada_w'], t['ada_b'])
        if stop == 'mod':
            return k
        with ExitStack() as keep:
            k.kT0_hi = keep.enter_context(nc.sbuf_tensor("kT0_hi", [P, NT * P], F32R))
            k.kT0_lo = keep.enter_context(nc.sbuf_tensor("kT0_lo", [P, NT * P], F32R))
            k.v0 = keep.enter_context(nc.sbuf_tensor("v0", [P, NT, A_KV], F32))
            project_even(nc, k, t['ev_w_in'][0], t['a_q_norm'][0], t['a_k_norm'][0], t['b_v_norm'][0], t['b_ws'][0],
                         t['b_bs'][0], t['k_rope'])
            if stop == 'pe':
                return k
            attend(nc, k, 0, t['ev_w_out'][0], None, None)
        if stop == 'at0':
            return k
        with ExitStack() as keep:
            moe(nc, k, keep, 0, t, NT)
            with Phase(nc, "cw") as ph:
                w = conv_weights(ph, t['od_w_in'][0])
                combine(nc, k, 0, NT, w)
                if stop == 'moe0':
                    return k
                project_conv(nc, k, w, t['d_dw'][0], t['d_dw_b'][0], t['d_ln_g'][0], t['d_ln_b'][0])
        if stop == 'conv':
            return k
        with ExitStack() as keep:
            k.kT1_hi = keep.enter_context(nc.sbuf_tensor("kT1_hi", [P, 4, NT * P], F32R))
            k.kT1_lo = keep.enter_context(nc.sbuf_tensor("kT1_lo", [P, 4, NT * P], F32R))
            k.v1 = keep.enter_context(nc.sbuf_tensor("v1", [P, NT, BW], F32))
            project_odd(nc, k, t['od_w_in'][0], t['c_q_norm'][0], t['c_k_norm'][0], t['c_rpb'][0])
            if stop == 'po':
                return k
            attend(nc, k, 1, t['od_w_out'][0], t['k_colmask'], t['k_rowmask'])
        if stop == 'at1':
            return k
        with ExitStack() as keep:
            moe(nc, k, keep, 1, t, LT)
            combine(nc, k, 1, LT)
    return k


def kernel(**inputs):
    import concourse.bacc as bacc
    from concourse.bass_utils import run_bass_kernel_spmd

    nc = bacc.Bacc("TRN2", target_bir_lowering=False, num_devices=1)
    arrays, t = {}, {}
    for name, a in [(n, np.ascontiguousarray(inputs[n])) for n in _INS] + list(constants().items()):
        arrays[f"in_{name}"] = a
        t[name] = nc.dram_tensor(f"in_{name}", a.shape, mybir.dt.from_np(a.dtype), kind="ExternalInput").ap()
    out = nc.dram_tensor("out_0", (1, SEQ, D), F32, kind="ExternalOutput").ap()
    build(nc, t, out)
    r = run_bass_kernel_spmd(nc, [arrays], core_ids=[0])
    return r.results[0]["out_0"]
```
